# Optimizing a Trainium2 kernel written in Bass

```python
import math
import jax, jax.numpy as jnp
from jax import lax
import numpy as np

D_MODEL = 1024
BATCH = 1
SEQ = 256
DEPTH = 2

N_MIXERS = 2
N_ATTN_LAYERS = (DEPTH + 1) // 2
N_CONV_LAYERS = DEPTH // 2
RMS_EPS = 1e-6

HEAD_DIM = 64
N_Q_HEADS = D_MODEL // HEAD_DIM
N_KV_HEADS = 4
GROUP = N_Q_HEADS // N_KV_HEADS
WINDOW = 128
ROT_DIM = HEAD_DIM // 4
ROPE_THETA = 500000.0
QKV_DIM = (N_Q_HEADS + 2 * N_KV_HEADS) * HEAD_DIM
NEG_INF = -1e30

CONV_WIDTH = 3

PEER_HEADS = 8
N_KEYS = 128
N_EXPERTS = N_KEYS * N_KEYS
PEER_TOPK = 16
QUERY_DIM = 256
QUERY_HALF = QUERY_DIM // 2
TOKEN_BLOCK = 128


def rmsnorm(x, gain):
    x32 = x.astype(jnp.float32)
    y = x32 * lax.rsqrt(jnp.mean(x32 * x32, axis=-1, keepdims=True) + RMS_EPS)
    return (y * gain.astype(jnp.float32)).astype(x.dtype)

def partial_rope(x, pos):
    half = ROT_DIM // 2
    freqs = ROPE_THETA ** (-jnp.arange(0, ROT_DIM, 2, dtype=jnp.float32) / ROT_DIM)
    ang = pos.astype(jnp.float32)[:, None] * freqs[None, :]
    cos = jnp.cos(ang)[None, :, None, :]
    sin = jnp.sin(ang)[None, :, None, :]
    x32 = x.astype(jnp.float32)
    x1, x2, rest = x32[..., :half], x32[..., half:ROT_DIM], x32[..., ROT_DIM:]
    out = jnp.concatenate([x1 * cos - x2 * sin, x2 * cos + x1 * sin, rest], axis=-1)
    return out.astype(x.dtype)

def sliding_window_attention(xn, w_qkv, q_gain, k_gain, sinks, w_o):
    B, S, _ = xn.shape
    nb = S // WINDOW
    qkv = xn @ w_qkv
    q_end = N_Q_HEADS * HEAD_DIM
    k_end = q_end + N_KV_HEADS * HEAD_DIM
    q = qkv[..., :q_end].reshape(B, S, N_Q_HEADS, HEAD_DIM)
    k = qkv[..., q_end:k_end].reshape(B, S, N_KV_HEADS, HEAD_DIM)
    v = qkv[..., k_end:].reshape(B, S, N_KV_HEADS, HEAD_DIM)
    q = rmsnorm(q, q_gain)
    k = rmsnorm(k, k_gain)
    pos = jnp.arange(S)
    q = partial_rope(q, pos)
    k = partial_rope(k, pos)

    qb = q.reshape(B, nb, WINDOW, N_KV_HEADS, GROUP, HEAD_DIM)
    pad = ((0, 0), (WINDOW, 0), (0, 0), (0, 0))
    kp = jnp.pad(k, pad).reshape(B, nb + 1, WINDOW, N_KV_HEADS, HEAD_DIM)
    vp = jnp.pad(v, pad).reshape(B, nb + 1, WINDOW, N_KV_HEADS, HEAD_DIM)
    kband = jnp.concatenate([kp[:, :-1], kp[:, 1:]], axis=2)
    vband = jnp.concatenate([vp[:, :-1], vp[:, 1:]], axis=2)

    scale = 1.0 / math.sqrt(HEAD_DIM)
    s = jnp.einsum('bnqhgd,bnkhd->bnhgqk', qb, kband).astype(jnp.float32) * scale
    qi = jnp.arange(WINDOW)[:, None]
    ki = jnp.arange(2 * WINDOW)[None, :]
    rel = WINDOW + qi - ki
    band = (rel >= 0) & (rel < WINDOW)
    blk = jnp.arange(nb)[:, None, None]
    valid = band[None] & (blk * WINDOW + ki[None] >= WINDOW)
    s = jnp.where(valid[None, :, None, None], s, NEG_INF)

    sink = sinks.astype(jnp.float32).reshape(N_KV_HEADS, GROUP)[None, None, :, :, None, None]
    sink = jnp.broadcast_to(sink, s.shape[:-1] + (1,))
    p = jax.nn.softmax(jnp.concatenate([s, sink], axis=-1), axis=-1)[..., :-1]
    o = jnp.einsum('bnhgqk,bnkhd->bnqhgd', p.astype(vband.dtype), vband)
    return o.reshape(B, S, N_Q_HEADS * HEAD_DIM) @ w_o

def short_gated_conv(xn, w_in, conv_w, w_out):
    B, S, D = xn.shape
    bcu = xn @ w_in
    gate_b = bcu[..., :D]
    gate_c = bcu[..., D:2 * D]
    u = bcu[..., 2 * D:]
    z = gate_c * u
    zp = jnp.pad(z, ((0, 0), (CONV_WIDTH - 1, 0), (0, 0)))
    conv = sum(conv_w[j] * zp[:, j:j + S] for j in range(CONV_WIDTH))
    return (gate_b * conv) @ w_out

def peer_ffn(xn, w_query, sub_keys, expert_u, expert_v):
    B, S, D = xn.shape
    T = B * S
    xt = xn.reshape(T, D)
    q = (xt @ w_query).reshape(T, PEER_HEADS, 2, QUERY_HALF)
    s = jnp.einsum('thpd,hpnd->thpn', q, sub_keys).astype(jnp.float32)
    s_top, i_top = lax.top_k(s, PEER_TOPK)
    cand = (s_top[:, :, 0, :, None] + s_top[:, :, 1, None, :]).reshape(T, PEER_HEADS, PEER_TOPK * PEER_TOPK)
    cand_idx = (i_top[:, :, 0, :, None] * N_KEYS + i_top[:, :, 1, None, :]).reshape(T, PEER_HEADS, PEER_TOPK * PEER_TOPK)
    g_s, sel = lax.top_k(cand, PEER_TOPK)
    idx = jnp.take_along_axis(cand_idx, sel, axis=-1)
    g = jax.nn.softmax(g_s, axis=-1)

    nblk = T // TOKEN_BLOCK

    def expert_block(args):
        xc, ic, gc = args
        u = jnp.take(expert_u, ic, axis=0)
        a = jnp.einsum('td,thkd->thk', xc, u).astype(jnp.float32)
        w = (gc * jax.nn.gelu(a, approximate=False)).astype(xc.dtype)
        v = jnp.take(expert_v, ic, axis=0)
        return jnp.einsum('thk,thkd->td', w, v)

    y = lax.map(expert_block, (xt.reshape(nblk, TOKEN_BLOCK, D),
                               idx.reshape(nblk, TOKEN_BLOCK, PEER_HEADS, PEER_TOPK),
                               g.reshape(nblk, TOKEN_BLOCK, PEER_HEADS, PEER_TOPK)))
    return y.reshape(B, S, D)

def first_inputs(seed: int = 0) -> dict:
    key = jax.random.key(seed)
    ks = jax.random.split(key, 16)
    D = D_MODEL
    nrm = jax.random.normal
    x = nrm(ks[0], (BATCH, SEQ, D), jnp.float32)
    norm_mix = 1.0 + 0.05 * nrm(ks[1], (DEPTH, D), jnp.float32)
    norm_ffn = 1.0 + 0.05 * nrm(ks[2], (DEPTH, D), jnp.float32)
    attn_w_qkv = nrm(ks[3], (N_ATTN_LAYERS, D, QKV_DIM), jnp.float32) * D ** -0.5
    attn_q_norm = 1.0 + 0.05 * nrm(ks[4], (N_ATTN_LAYERS, HEAD_DIM), jnp.float32)
    attn_k_norm = 1.0 + 0.05 * nrm(ks[5], (N_ATTN_LAYERS, HEAD_DIM), jnp.float32)
    attn_sinks = 0.5 * nrm(ks[6], (N_ATTN_LAYERS, N_Q_HEADS), jnp.float32)
    attn_w_o = nrm(ks[7], (N_ATTN_LAYERS, N_Q_HEADS * HEAD_DIM, D), jnp.float32) * (N_Q_HEADS * HEAD_DIM) ** -0.5
    conv_w_in = nrm(ks[8], (N_CONV_LAYERS, D, 3 * D), jnp.float32) * D ** -0.5
    conv_w = nrm(ks[9], (N_CONV_LAYERS, CONV_WIDTH, D), jnp.float32) * CONV_WIDTH ** -0.5
    conv_w_out = nrm(ks[10], (N_CONV_LAYERS, D, D), jnp.float32) * D ** -0.5
    peer_w_query = nrm(ks[11], (DEPTH, D, PEER_HEADS * QUERY_DIM), jnp.float32) * D ** -0.5
    peer_sub_keys = nrm(ks[12], (DEPTH, PEER_HEADS, 2, N_KEYS, QUERY_HALF), jnp.float32) * QUERY_HALF ** -0.5
    peer_u = nrm(ks[13], (DEPTH, N_EXPERTS, D), jnp.float32) * D ** -0.5
    peer_v = nrm(ks[14], (DEPTH, N_EXPERTS, D), jnp.float32) * (PEER_HEADS * PEER_TOPK) ** -0.5
    return {"x": x, "norm_mix": norm_mix, "norm_ffn": norm_ffn,
            "attn_w_qkv": attn_w_qkv, "attn_q_norm": attn_q_norm, "attn_k_norm": attn_k_norm,
            "attn_sinks": attn_sinks, "attn_w_o": attn_w_o,
            "conv_w_in": conv_w_in, "conv_w": conv_w, "conv_w_out": conv_w_out,
            "peer_w_query": peer_w_query, "peer_sub_keys": peer_sub_keys,
            "peer_u": peer_u, "peer_v": peer_v}

def first_block(x, norm_mix, norm_ffn, attn_w_qkv, attn_q_norm, attn_k_norm, attn_sinks, attn_w_o,
              conv_w_in, conv_w, conv_w_out, peer_w_query, peer_sub_keys, peer_u, peer_v):
    for i in range(DEPTH):
        h = rmsnorm(x, norm_mix[i])
        j = i // N_MIXERS
        if i % N_MIXERS == 0:
            x = x + sliding_window_attention(h, attn_w_qkv[j], attn_q_norm[j], attn_k_norm[j],
                                             attn_sinks[j], attn_w_o[j])
        else:
            x = x + short_gated_conv(h, conv_w_in[j], conv_w[j], conv_w_out[j])
        h = rmsnorm(x, norm_ffn[i])
        x = x + peer_ffn(h, peer_w_query[i], peer_sub_keys[i], peer_u[i], peer_v[i])
    return x


DEPTH_2 = 1

A_HEADS = 8
A_HEAD_DIM = 64
A_WIDTH = A_HEADS * A_HEAD_DIM
MOBA_BLOCK = 256
MOBA_TOPK = 3
MOBA_Q_CHUNK = 32
B_HEADS = 8
B_NOPE = 64
B_ROPE = 32
B_V = 64
B_WIDTH = B_HEADS * B_V
Q_LORA = 256
KV_LORA = 128
MLA_Q_BLOCK = 128
PEER_NKEYS = 128
PEER_EXPERTS = PEER_NKEYS * PEER_NKEYS
PEER_HALF = 128
PEER_QDIM = 2 * PEER_HALF
PEER_TOKEN_CHUNK = 128
ROPE_THETA_2 = 10000.0
IN_WIDTHS = (A_WIDTH, A_WIDTH, A_WIDTH, Q_LORA, KV_LORA, B_ROPE, D_MODEL, D_MODEL)
IN_TOTAL = 3 * A_WIDTH + Q_LORA + KV_LORA + B_ROPE + 2 * D_MODEL


def rms_norm(x, g):
    xf = x.astype(jnp.float32)
    y = xf * lax.rsqrt(jnp.mean(xf * xf, axis=-1, keepdims=True) + RMS_EPS)
    return (y * g.astype(jnp.float32)).astype(x.dtype)

def rope_tables(positions, dim, dtype):
    inv_freq = ROPE_THETA_2 ** (-jnp.arange(0, dim, 2, dtype=jnp.float32) / dim)
    ang = positions.astype(jnp.float32)[..., None] * inv_freq
    return jnp.cos(ang)[:, :, None, :].astype(dtype), jnp.sin(ang)[:, :, None, :].astype(dtype)

def apply_rope(x, cos, sin):
    x1, x2 = jnp.split(x, 2, axis=-1)
    return jnp.concatenate([x1 * cos - x2 * sin, x2 * cos + x1 * sin], axis=-1)

def moba_attention(q, k, v):
    B, S, H, dh = q.shape
    nb = -(-S // MOBA_BLOCK)
    pad = nb * MOBA_BLOCK - S
    k_eff = min(MOBA_TOPK, nb)
    scale = 1.0 / math.sqrt(dh)
    qt = q.transpose(0, 2, 1, 3)
    kt = jnp.pad(k.transpose(0, 2, 1, 3), ((0, 0), (0, 0), (0, pad), (0, 0)))
    vt = jnp.pad(v.transpose(0, 2, 1, 3), ((0, 0), (0, 0), (0, pad), (0, 0)))
    kb = kt.reshape(B, H, nb, MOBA_BLOCK, dh)
    vb = vt.reshape(B, H, nb, MOBA_BLOCK, dh)
    k_mean = jnp.mean(kb.astype(jnp.float32), axis=3)
    b_ix = jnp.arange(B)[:, None, None, None]
    h_ix = jnp.arange(H)[None, :, None, None]
    n_chunks = S // MOBA_Q_CHUNK

    def chunk(ci):
        start = ci * MOBA_Q_CHUNK
        blk = start // MOBA_BLOCK
        qc = lax.dynamic_slice_in_dim(qt, start, MOBA_Q_CHUNK, axis=2)
        gate = jnp.einsum('bhqd,bhnd->bhqn', qc.astype(jnp.float32), k_mean)
        gate = jnp.where(jnp.arange(nb) < blk, gate, -jnp.inf)
        _, sel = lax.top_k(gate, k_eff)
        sel_valid = jnp.arange(k_eff) < blk
        k_sel = kb[b_ix, h_ix, sel]
        v_sel = vb[b_ix, h_ix, sel]
        s_sel = jnp.einsum('bhqd,bhqtkd->bhqtk', qc, k_sel).astype(jnp.float32) * scale
        s_sel = jnp.where(sel_valid[:, None], s_sel, -jnp.inf)
        s_sel = s_sel.reshape(B, H, MOBA_Q_CHUNK, k_eff * MOBA_BLOCK)
        k_own = lax.dynamic_index_in_dim(kb, blk, axis=2, keepdims=False)
        v_own = lax.dynamic_index_in_dim(vb, blk, axis=2, keepdims=False)
        s_own = jnp.einsum('bhqd,bhkd->bhqk', qc, k_own).astype(jnp.float32) * scale
        q_pos = start + jnp.arange(MOBA_Q_CHUNK)
        k_pos = blk * MOBA_BLOCK + jnp.arange(MOBA_BLOCK)
        s_own = jnp.where(k_pos[None, :] <= q_pos[:, None], s_own, -jnp.inf)
        p = jax.nn.softmax(jnp.concatenate([s_sel, s_own], axis=-1), axis=-1).astype(v.dtype)
        p_sel = p[..., :k_eff * MOBA_BLOCK].reshape(B, H, MOBA_Q_CHUNK, k_eff, MOBA_BLOCK)
        p_own = p[..., k_eff * MOBA_BLOCK:]
        return (jnp.einsum('bhqtk,bhqtkd->bhqd', p_sel, v_sel)
                + jnp.einsum('bhqk,bhkd->bhqd', p_own, v_own))

    out = lax.map(chunk, jnp.arange(n_chunks))
    return out.transpose(1, 0, 3, 2, 4).reshape(B, S, H * dh)

def causal_attention_blocks(q, k, v, scale):
    B, H, S, _ = q.shape
    dv = v.shape[-1]
    k_pos = jnp.arange(S)

    def block(bi):
        qb = lax.dynamic_slice_in_dim(q, bi * MLA_Q_BLOCK, MLA_Q_BLOCK, axis=2)
        s = jnp.einsum('bhqd,bhkd->bhqk', qb, k).astype(jnp.float32) * scale
        q_pos = bi * MLA_Q_BLOCK + jnp.arange(MLA_Q_BLOCK)
        s = jnp.where(k_pos[None, :] <= q_pos[:, None], s, -jnp.inf)
        p = jax.nn.softmax(s, axis=-1).astype(v.dtype)
        return jnp.einsum('bhqk,bhkd->bhqd', p, v)

    out = lax.map(block, jnp.arange(S // MLA_Q_BLOCK))
    return out.transpose(1, 0, 3, 2, 4).reshape(B, S, H * dv)

def mla_attention(c_q, c_kv, k_pe, q_norm_g, w_q_up, kv_norm_g, w_kv_up, cos_b, sin_b):
    B, S, _ = c_q.shape
    q = (rms_norm(c_q, q_norm_g) @ w_q_up).reshape(B, S, B_HEADS, B_NOPE + B_ROPE)
    q_nope, q_pe = q[..., :B_NOPE], q[..., B_NOPE:]
    q_pe = apply_rope(q_pe, cos_b, sin_b)
    kv = (rms_norm(c_kv, kv_norm_g) @ w_kv_up).reshape(B, S, B_HEADS, B_NOPE + B_V)
    k_nope, v = kv[..., :B_NOPE], kv[..., B_NOPE:]
    k_pe = apply_rope(k_pe[:, :, None, :], cos_b, sin_b)
    k_pe = jnp.broadcast_to(k_pe, (B, S, B_HEADS, B_ROPE))
    q_full = jnp.concatenate([q_nope, q_pe], axis=-1).transpose(0, 2, 1, 3)
    k_full = jnp.concatenate([k_nope, k_pe], axis=-1).transpose(0, 2, 1, 3)
    v = v.transpose(0, 2, 1, 3)
    return causal_attention_blocks(q_full, k_full, v, 1.0 / math.sqrt(B_NOPE + B_ROPE))

def peer_ffn_2(h, w_query, sub_keys_1, sub_keys_2, expert_u, expert_v):
    B, S, D = h.shape
    T = B * S
    hc = h.reshape(T // PEER_TOKEN_CHUNK, PEER_TOKEN_CHUNK, D)

    def chunk(xc):
        q = (xc @ w_query).reshape(PEER_TOKEN_CHUNK, PEER_HEADS, 2, PEER_HALF)
        s1 = jnp.einsum('thd,hnd->thn', q[:, :, 0], sub_keys_1).astype(jnp.float32)
        s2 = jnp.einsum('thd,hnd->thn', q[:, :, 1], sub_keys_2).astype(jnp.float32)
        v1, i1 = lax.top_k(s1, PEER_TOPK)
        v2, i2 = lax.top_k(s2, PEER_TOPK)
        cand = (v1[..., :, None] + v2[..., None, :]).reshape(PEER_TOKEN_CHUNK, PEER_HEADS, PEER_TOPK * PEER_TOPK)
        cand_idx = (i1[..., :, None] * PEER_NKEYS + i2[..., None, :]).reshape(PEER_TOKEN_CHUNK, PEER_HEADS, PEER_TOPK * PEER_TOPK)
        best, pos = lax.top_k(cand, PEER_TOPK)
        idx = jnp.take_along_axis(cand_idx, pos, axis=-1)
        g = jax.nn.softmax(best, axis=-1)
        u = expert_u[idx]
        act = jax.nn.gelu(jnp.einsum('td,thkd->thk', xc, u).astype(jnp.float32), approximate=False)
        w = (g * act).astype(h.dtype)
        return jnp.einsum('thk,thkd->td', w, expert_v[idx])

    return lax.map(chunk, hc).reshape(B, S, D)

def second_inputs(seed: int = 0) -> dict:
    key = jax.random.key(seed)
    ks = jax.random.split(key, 20)
    f32 = jnp.float32
    L = DEPTH_2

    def nrm(k, shape, scale):
        return jax.random.normal(k, shape, f32) * scale

    def gain(k, shape):
        return 1.0 + 0.02 * jax.random.normal(k, shape, f32)

    x = jax.random.normal(ks[0], (BATCH, SEQ, D_MODEL), f32)
    positions = jnp.broadcast_to(jnp.arange(SEQ, dtype=jnp.int32), (BATCH, SEQ))
    return {
        "x": x,
        "positions": positions,
        "mix_norm_g": gain(ks[1], (L, D_MODEL)),
        "w_in": nrm(ks[2], (L, D_MODEL, IN_TOTAL), D_MODEL ** -0.5),
        "q_norm_g": gain(ks[3], (L, Q_LORA)),
        "w_q_up": nrm(ks[4], (L, Q_LORA, B_HEADS * (B_NOPE + B_ROPE)), Q_LORA ** -0.5),
        "kv_norm_g": gain(ks[5], (L, KV_LORA)),
        "w_kv_up": nrm(ks[6], (L, KV_LORA, B_HEADS * (B_NOPE + B_V)), KV_LORA ** -0.5),
        "w_branch_a": nrm(ks[7], (L, A_WIDTH, D_MODEL), A_WIDTH ** -0.5),
        "w_branch_b": nrm(ks[8], (L, B_WIDTH, D_MODEL), B_WIDTH ** -0.5),
        "w_out": nrm(ks[9], (L, D_MODEL, D_MODEL), D_MODEL ** -0.5),
        "ffn_norm_g": gain(ks[10], (L, D_MODEL)),
        "w_peer_query": nrm(ks[11], (L, D_MODEL, PEER_HEADS * PEER_QDIM), D_MODEL ** -0.5),
        "peer_sub_keys_1": nrm(ks[12], (L, PEER_HEADS, PEER_NKEYS, PEER_HALF), PEER_HALF ** -0.5),
        "peer_sub_keys_2": nrm(ks[13], (L, PEER_HEADS, PEER_NKEYS, PEER_HALF), PEER_HALF ** -0.5),
        "peer_expert_u": nrm(ks[14], (L, PEER_EXPERTS, D_MODEL), D_MODEL ** -0.5),
        "peer_expert_v": nrm(ks[15], (L, PEER_EXPERTS, D_MODEL), (PEER_HEADS * PEER_TOPK) ** -0.5),
        "final_norm_g": gain(ks[16], (D_MODEL,)),
    }

def second_block(x, positions, mix_norm_g, w_in, q_norm_g, w_q_up, kv_norm_g, w_kv_up,
              w_branch_a, w_branch_b, w_out, ffn_norm_g, w_peer_query, peer_sub_keys_1,
              peer_sub_keys_2, peer_expert_u, peer_expert_v, final_norm_g):
    B, S, _ = x.shape
    cos_a, sin_a = rope_tables(positions, A_HEAD_DIM, x.dtype)
    cos_b, sin_b = rope_tables(positions, B_ROPE, x.dtype)
    splits = [sum(IN_WIDTHS[:i + 1]) for i in range(len(IN_WIDTHS) - 1)]
    for layer in range(DEPTH_2):
        h = rms_norm(x, mix_norm_g[layer])
        proj = h @ w_in[layer]
        q_a, k_a, v_a, c_q, c_kv, k_pe, gate_a, gate_b = jnp.split(proj, splits, axis=-1)
        q_a = apply_rope(q_a.reshape(B, S, A_HEADS, A_HEAD_DIM), cos_a, sin_a)
        k_a = apply_rope(k_a.reshape(B, S, A_HEADS, A_HEAD_DIM), cos_a, sin_a)
        v_a = v_a.reshape(B, S, A_HEADS, A_HEAD_DIM)
        y_a = moba_attention(q_a, k_a, v_a)
        y_b = mla_attention(c_q, c_kv, k_pe, q_norm_g[layer], w_q_up[layer],
                            kv_norm_g[layer], w_kv_up[layer], cos_b, sin_b)
        merged = (jax.nn.sigmoid(gate_a) * (y_a @ w_branch_a[layer])
                  + jax.nn.sigmoid(gate_b) * (y_b @ w_branch_b[layer]))
        x = x + merged @ w_out[layer]
        x = x + peer_ffn_2(rms_norm(x, ffn_norm_g[layer]), w_peer_query[layer],
                         peer_sub_keys_1[layer], peer_sub_keys_2[layer],
                         peer_expert_u[layer], peer_expert_v[layer])
    return rms_norm(x, final_norm_g)


def setup_inputs(seed=0):
    out = dict(first_inputs(seed))
    for name, value in second_inputs(seed + 1).items():
        if name != "x":
            out[name + "_2"] = value
    return out


def reference(
    x, norm_mix, norm_ffn, attn_w_qkv, attn_q_norm, attn_k_norm, attn_sinks, attn_w_o,
    conv_w_in, conv_w, conv_w_out, peer_w_query, peer_sub_keys, peer_u, peer_v, positions_2,
    mix_norm_g_2, w_in_2, q_norm_g_2, w_q_up_2, kv_norm_g_2, w_kv_up_2, w_branch_a_2,
    w_branch_b_2, w_out_2, ffn_norm_g_2, w_peer_query_2, peer_sub_keys_1_2, peer_sub_keys_2_2,
    peer_expert_u_2, peer_expert_v_2, final_norm_g_2,
):
    x = first_block(
        x, norm_mix, norm_ffn, attn_w_qkv, attn_q_norm, attn_k_norm, attn_sinks, attn_w_o,
        conv_w_in, conv_w, conv_w_out, peer_w_query, peer_sub_keys, peer_u, peer_v,
    )
    return second_block(
        x, positions_2, mix_norm_g_2, w_in_2, q_norm_g_2, w_q_up_2, kv_norm_g_2, w_kv_up_2,
        w_branch_a_2, w_branch_b_2, w_out_2, ffn_norm_g_2, w_peer_query_2, peer_sub_keys_1_2,
        peer_sub_keys_2_2, peer_expert_u_2, peer_expert_v_2, final_norm_g_2,
    )


_drawn_inputs = setup_inputs


def setup_inputs(seed=0):
    import zlib

    import numpy as np

    out = dict(_drawn_inputs(seed))
    spreads = {}
    factors = {'norm_ffn': 3.209,
     'attn_q_norm': 3.907,
     'attn_k_norm': 3.449,
     'attn_sinks': 3.59,
     'mix_norm_g_2': 8.0,
     'q_norm_g_2': 8.0,
     'kv_norm_g_2': 8.0,
     'ffn_norm_g_2': 44.783,
     'final_norm_g_2': 7.45}
    for name, (base, spread) in spreads.items():
        noise = np.random.default_rng([zlib.crc32(name.encode()), seed]).standard_normal(out[name].shape)
        drawn = base * np.exp(spread * noise) if base else spread * noise
        out[name] = __import__('jax').numpy.asarray(drawn.astype(out[name].dtype))
    for name, factor in factors.items():
        out[name] = (out[name] * factor).astype(out[name].dtype)
    return out
```

```python
from contextlib import ExitStack

import numpy as np

import concourse.bass as bass
from concourse import mybir

F32 = mybir.dt.float32
U32 = mybir.dt.uint32
I32 = mybir.dt.int32
ACT = mybir.ActivationFunctionType
ALU = mybir.AluOpType
AXX = mybir.AxisListType.X

P = 128
D = 1024
KT = D // P
TILES = 2
LAYERS = 3
STEPS = LAYERS * TILES
EPS = 1e-6
NEG = -1e30

N_KEYS = 128
TOPK = 16
PEER_HEADS = 8
SLOTS = PEER_HEADS * TOPK
GROUP = 2
GROUPS = SLOTS // GROUP
PAIR = 2 * TOPK // GROUP
SPREAD = GROUPS - 1
MOVE_AT = 0
TURN = 8
BY_VECTOR = (1, 3, 4, 6, 7)
RING = 10
DIAGS = 6
ACOLS = 16

BLK = 512
WBLK = KT * BLK

PI = float(np.float32(np.pi))
TWO_PI = 2.0 * np.pi
C1 = 6.28125
C2 = float(np.floor((TWO_PI - C1) * 2.0 ** 22) / 2.0 ** 22)
C3 = float(np.float32(TWO_PI - C1 - C2))
ROUND = 1.5 * 2.0 ** 23


def layer(s):
    return s // TILES


def tile(s):
    return s % TILES


W_BLOCKS = [
    [("qkv0", WBLK), ("qkv1", WBLK), ("qkv2", WBLK), ("out0", WBLK), ("out1", WBLK)],
    [(n, WBLK) for n in ("c0", "u0", "c1", "u1", "b0", "b1", "out0", "out1")],
    [("q", WBLK), ("k", WBLK), ("v", WBLK), ("lat", KT * 416), ("ga0", WBLK), ("ga1", WBLK),
     ("gb0", WBLK), ("gb1", WBLK), ("ups", 2 * 768 + 1024), ("bra", WBLK), ("brb", WBLK),
     ("out0", WBLK), ("out1", WBLK)],
]
W_BLOCKS = [b + [(f"q{i}", WBLK) for i in range(4)] for b in W_BLOCKS]
W_BASE = [sum(len(b) for b in W_BLOCKS[:i]) for i in range(LAYERS)]

HEADS = {"win": 16, "moba": 8, "mla": 8}
SCALE = {"win": 0.125, "moba": 0.125, "mla": float(96 ** -0.5)}
PARTS = [["win"], [], ["moba", "mla"]]


def heads_per_chunk(s):
    return BLK // (P * (tile(s) + 1))


def chunks(s, part):
    return HEADS[part] // heads_per_chunk(s)


def chunk_heads(s, part, c):
    hg = heads_per_chunk(s)
    if part == "mla":
        return slice(c * hg, (c + 1) * hg, 1)
    first = c % 2 + 2 * hg * (c // 2)
    return slice(first, first + 2 * hg - 1, 2)


def acc_uses(s):
    if layer(s) == 0:
        mixer = [("qkv0", "act"), ("qkv1", "act"), ("qkv2", "act"), ("o_win0", "dve"), ("o_win1", "dve"),
                 ("out0", "dve"), ("out1", "dve")]
    elif layer(s) == 1:
        mixer = [("c0", "act"), ("u0", "dve"), ("c1", "act"), ("u1", "dve"), ("b0", "dve"), ("b1", "dve"),
                 ("out0", "dve"), ("out1", "dve")]
    else:
        mixer = [(n, "act") for n in ("q", "k", "v", "lat", "ga0", "ga1", "gb0", "gb1")]
        mixer += [("o_moba0", "dve")] + [(n, "act") for n in ("uq0", "uq1", "uk", "uv")] + [("o_mla0", "dve")]
        mixer += [(n, "dve") for n in ("bra0", "brb0", "bra1", "brb1", "out0", "out1")]
    return mixer + [(f"q{i}", "act") for i in range(4)]


def transposes(s):
    out = ["mix0", "mix1"]
    for part in PARTS[layer(s)]:
        out += {"win": ["win_q0", "win_q1", "win_k"], "moba": ["moba_q", "moba_k"],
                "mla": ["lat", "mla_q0", "mla_q1", "mla_k0", "mla_k1"]}[part]
        out += [f"{part}_p{c}" for c in range(chunks(s, part))]
        out += {"win": ["win_o0", "win_o1"], "moba": [], "mla": ["o0", "o1"]}[part]
    if layer(s) == 2:
        out += ["mrg0", "mrg1"]
    return out + ["ffn0", "ffn1"]


def score_uses(s):
    return [f"{part}_s{c}" for part in PARTS[layer(s)] for c in range(chunks(s, part))] + [f"key{b}" for b in range(4)]


def pieces(s):
    def attention(part):
        return [f"{part}_chunk{c}" for c in range(chunks(s, part) + 1)] + [f"{part}_end"]

    if layer(s) == 0:
        mixer = ["mix_stat", "mix_T", "qkv0", "qkv1", "qkv2", "qk_norm", "qk_T"] + attention("win")
        mixer += ["win_oT", "out0", "out1"]
    elif layer(s) == 1:
        mixer = ["mix_stat", "mix_T", "c0", "u0", "c1", "u1", "b0", "b1", "out0", "out1"]
    else:
        mixer = ["mix_stat", "mix_T", "q", "k", "v", "lat", "moba_rope", "ga0", "moba_T", "ga1", "gb0", "gb1"]
        mixer += attention("moba") + ["lat_norm", "lat_T", "uq0", "uq1", "uk", "uv", "mla_rope", "mla_T"]
        mixer += attention("mla") + ["oT", "br0", "br1", "mrg_T", "out0", "out1"]
    return mixer + ["ffn_stat", "ffn_T"] + [x for b in range(5) for x in ([f"query{b}"] + ([f"top{b - 1}"] if b else []))]


COST = {"top": 11.7, "chunk": 2.2, "rope": 6.7, "norm": 1.8, "turn": 2.0, "end": 3.8, "product": 12.3}


def cost(p):
    if p.startswith("top"):
        return COST["top"]
    if "_chunk" in p:
        return COST["chunk"]
    if p in ("qk_norm", "moba_rope", "mla_rope", "u0", "u1"):
        return COST["rope"]
    if p.endswith(("_stat", "lat_norm")):
        return COST["norm"]
    if p.endswith("_end"):
        return COST["end"]
    if p.endswith(("_T", "oT")):
        return COST["turn"]
    return COST["product"]


def schedule():
    out = []
    first = pieces(0)
    ready = first.index("top0") + 1
    out += [("D", 0, p) for p in first[:ready]]
    waiting = [("D", 0, p) for p in first[ready:]]
    for s in range(STEPS):
        todo = waiting + ([("D", s + 1, p) for p in pieces(s + 1)] if s + 1 < STEPS else [])
        waiting = []
        total = sum(cost(p) for _, _, p in todo)
        spent = 0.0
        for g in range(GROUPS):
            out.append(("G", s, g))
            if g == MOVE_AT and s > 0:
                out.append(("X", s - 1, 0))
            while todo and (g >= MOVE_AT or s == 0) and spent + cost(todo[0][2]) / 2 < total * (g + 1) / SPREAD:
                spent += cost(todo[0][2])
                out.append(todo.pop(0))
        out += todo
    out.append(("X", STEPS - 1, 0))
    return out


SCHEDULE = schedule()


class Signal:

    def __init__(self, sem, per_step):
        self.sem, self.value, n = sem, {}, 0
        for s, labels in enumerate(per_step):
            for label in labels:
                n += 1
                self.value[s, label] = n

    def count(self, s, label):
        return self.value[s, label]


def build(nc, xin, wts, keys, gains, small, sinks, convw, pos, rope0, invf, iota, ident, masks, uv, out):
    ctx = ExitStack()
    with ctx:
        def sb(name, shape, dt=F32):
            return ctx.enter_context(nc.sbuf_tensor(name, shape, dt))

        def ps(name):
            return ctx.enter_context(nc.psum_tensor(name, [P, BLK], F32))

        def sem(name):
            return ctx.enter_context(nc.semaphore(name))

        steps = range(STEPS)

        ring = sb("ring", [P, RING, 2 * D])
        wbuf = sb("wbuf", [P, 2, WBLK])
        kbuf = sb("kbuf", [P, 2, BLK])
        x = sb("x", [P, TILES, D])
        h = sb("h", [P, TILES, D])
        fT = sb("fT", [P, KT, P])
        gain = sb("gain", [P, D])
        smallr = sb("smallr", [P, 512])
        sink = sb("sink", [P, 16])
        cw = sb("cw", [P, KT, 3])
        posi = sb("posi", [P, TILES], I32)
        posf = sb("posf", [P, TILES])
        rc = sb("rc", [P, TILES, 16])
        inv = sb("inv", [P, 48])
        cosr = sb("cosr", [P, TILES, 48])
        sinr = sb("sinr", [P, TILES, 48])
        iota_s = sb("iota_s", [P, TOPK])
        id_s = sb("id_s", [P, P])
        mask_s = sb("mask_s", [P, 4, P])
        epsc = sb("epsc", [P, 1])

        a = sb("a", [P, ACOLS])
        ge = sb("ge", [P, ACOLS])
        wgt = sb("wgt", [P, ACOLS])
        diag = sb("diag", [P, DIAGS, P])
        idx = sb("idx", [P, TILES, SLOTS], U32)
        gate = sb("gate", [P, TILES, SLOTS])

        big = sb("big", [P, 2 * D])
        qk = sb("qk", [P, 1440])
        oM = sb("oM", [P, D])
        qT = sb("qT", [P, KT, P])
        caches = sb("caches", [P, 5120])
        tmp = sb("tmp", [P, 1280])
        sm = sb("sm", [P, 2, BLK])
        pT = sb("pT", [P, 2, BLK])
        st = sb("st", [P, 16])
        r20 = sb("r20", [P, 40])
        mx = sb("mx", [P, 16])
        nmx = sb("nmx", [P, 16])
        den = sb("den", [P, 16])
        rden = sb("rden", [P, 16])
        esink = sb("esink", [P, 16])
        tv = sb("tv", [P, 4, TOPK])
        ti = sb("ti", [P, 4, TOPK], U32)
        tf = sb("tf", [P, 4, TOPK])
        best = sb("best", [P, 2, TOPK])
        nbest = sb("nbest", [P, 2])
        bsum = sb("bsum", [P, 2])
        posu = sb("posu", [P, 2, 2 * TOPK], U32)

        lat = qk[:, 1024:1440]
        ang = oM[:, 0:96].rearrange("p (t n) -> p t n", t=TILES)
        angk = oM[:, 96:192].rearrange("p (t n) -> p t n", t=TILES)
        queryT = qT[:, :, :].rearrange("p (b a) n -> p b (a n)", b=2)
        swork = sm[:, 0, :]
        isel = sm[:, 0, 0:4 * TOPK].rearrange("p (a n) -> p a n", a=2)
        posn = sm[:, 0, 4 * TOPK:8 * TOPK].rearrange("p (a n) -> p a n", a=2)
        cand = sm[:, 1, :].rearrange("p (a n) -> p a n", a=2)
        hot = pT[:, :, :].rearrange("p b n -> p (b n)").rearrange("p (a b c) -> p a b c", a=2, c=TOPK)

        c0_kT = caches[:, 0:512].rearrange("p (a n) -> p a n", a=2)
        c0_v = caches[:, 512:1024].rearrange("p (t n) -> p t n", t=TILES)
        z = caches[:, 0:KT * (P + 2)].rearrange("p (c n) -> p c n", c=KT)
        c2_kaT = caches[:, 0:1024].rearrange("p (a n) -> p a n", a=4)
        c2_va = caches[:, 1024:2048].rearrange("p (t n) -> p t n", t=TILES)
        c2_kbT = caches[:, 2048:4096].rearrange("p (a n) -> p a n", a=8)
        c2_vb = caches[:, 4096:5120].rearrange("p (t n) -> p t n", t=TILES)
        kfull = tmp[:, 0:768].rearrange("p (h n) -> p h n", h=8)

        y = [ps("y0"), ps("y1")]
        acc = [ps("acc0"), ps("acc1")]
        tp = [ps("tp0"), ps("tp1")]
        sc = [ps("sc0"), ps("sc1")]

        norms = [["mix", "ffn"] for s in steps]
        finals = [["final"] if layer(s) == LAYERS - 1 else [] for s in steps]
        const_in = sem("const_in")
        x_in = sem("x_in")
        w_in = [sem("w_in0"), sem("w_in1")]
        k_in = [sem("k_in0"), sem("k_in1")]
        gain_in = sem("gain_in")
        row_in = [sem(f"row_in{i}") for i in range(RING)]
        stored = sem("stored")
        dve_step = sem("dve_step")
        act_step = sem("act_step")
        acc_done = Signal(sem("acc_done"), [[n for n, _ in acc_uses(s)] for s in steps])
        acc_out = {e: Signal(sem(f"acc_out_{e}"), [[n for n, f in acc_uses(s) if f == e] for s in steps])
                   for e in ("act", "dve")}
        tp_done = Signal(sem("tp_done"), [transposes(s) for s in steps])
        tp_copied = Signal(sem("tp_copied"), [transposes(s) for s in steps])
        sc_done = Signal(sem("sc_done"), [score_uses(s) for s in steps])
        sc_read = Signal(sem("sc_read"), [score_uses(s) for s in steps])
        x_moved = Signal(sem("x_moved"), [["y"]] * STEPS)
        sq_ready = Signal(sem("sq_ready"), norms)
        h_ready = Signal(sem("h_ready"), norms)
        last_sq = Signal(sem("last_sq"), finals)
        out_ready = Signal(sem("out_ready"), finals)
        dve_at = Signal(sem("dve_at"), [
            {0: ["qk_sq", "qk_norm", "win_den"], 1: [],
             2: ["lat_sq", "moba_rope", "lat_norm", "mla_rope", "mrg"]}[layer(s)] for s in steps])
        act_at = Signal(sem("act_at"), [
            {0: ["qk_rms", "win_esink"], 1: [], 2: ["lat_rms"]}[layer(s)] for s in steps])
        probs = Signal(sem("probs"), [[f"{p}_s{c}" for p in PARTS[layer(s)] for c in range(chunks(s, p))] for s in steps])
        max_done = Signal(sem("max_done"), [[f"{p}_s{c}" for p in PARTS[layer(s)] for c in range(chunks(s, p))] for s in steps])
        best_done = Signal(sem("best_done"), [range(4)] * STEPS)
        gate_exp = Signal(sem("gate_exp"), [range(4)] * STEPS)
        idx_ready = Signal(sem("idx_ready"), [range(4)] * STEPS)
        dots = Signal(sem("dots"), [range(GROUPS)] * STEPS)
        by_tensor = [k for k in range(SLOTS) if k % TURN not in BY_VECTOR]
        by_vector = [k for k in range(SLOTS) if k % TURN in BY_VECTOR]
        diags = Signal(sem("diags"), [by_tensor] * STEPS)
        y_slot = Signal(sem("y_slot"), [by_tensor] * STEPS)
        x_slot = Signal(sem("x_slot"), [by_vector] * STEPS)
        weights_at = Signal(sem("weights_at"), [range(GROUPS)] * STEPS)
        trig_arg = sem("trig_arg")
        trig = sem("trig")

        N_CONST = 9
        w_order = [(s, i) for s in steps for i in range(len(W_BLOCKS[layer(s)]))]
        w_index = {(s, W_BLOCKS[layer(s)][i][0]): n for n, (s, i) in enumerate(w_order)}
        acc_order = [(s, n, e) for s in steps for n, e in acc_uses(s)]
        acc_index = {(s, n): i for i, (s, n, _) in enumerate(acc_order)}
        tp_order = [(s, n) for s in steps for n in transposes(s)]
        tp_index = {k: i for i, k in enumerate(tp_order)}
        sc_order = [(s, n) for s in steps for n in score_uses(s)]
        sc_index = {k: i for i, k in enumerate(sc_order)}
        at_order = [(s, f"{p}_s{c}") for s in steps for p in PARTS[layer(s)] for c in range(chunks(s, p))]
        at_index = {k: i for i, k in enumerate(at_order)}

        def acc_bank(s, name):
            return acc[acc_index[s, name] % 2]

        def tp_bank(s, name):
            return tp[tp_index[s, name] % 2]

        def sc_bank(s, name):
            return sc[sc_index[s, name] % 2]

        def keys_len(s):
            return P * (tile(s) + 1)

        def slot_done(engine, n):
            s, k = divmod(n, SLOTS)
            sig = x_slot if k % TURN in BY_VECTOR else y_slot
            engine.wait_ge(sig.sem, sig.count(s, k))

        block = ctx.enter_context(nc.Block())

        @block.sync
        def _(sp):
            for t in range(TILES):
                sp.dma_start(x[:, t, :], xin[t * P:(t + 1) * P, :]).then_inc(x_in, 16)
            for dst, src in ((smallr[:], small.broadcast_to([P, 512])), (sink[:], sinks.broadcast_to([P, 16])),
                             (cw[:], convw), (posi[:], pos), (rc[:], rope0),
                             (inv[:], invf.broadcast_to([P, 48])), (iota_s[:], iota.broadcast_to([P, TOPK])),
                             (id_s[:], ident), (mask_s[:], masks)):
                sp.dma_start(dst, src).then_inc(const_in, 16)

            def load_gain(n, row):
                if n:
                    s, which = norm_order[n - 1]
                    sp.wait_ge(h_ready.sem, h_ready.count(s, which))
                sp.dma_start(gain[:], gains[row:row + 1, :].broadcast_to([P, D])).then_inc(gain_in, 16)

            norm_order = [(s, which) for s in steps for which in ("mix", "ffn")]
            last_use = {"ups": "uv", "bra": "bra1", "brb": "brb1"}
            n_gain = 0
            for n, (s, i) in enumerate(w_order):
                name, size = W_BLOCKS[layer(s)][i]
                if i == 0:
                    load_gain(n_gain, 2 * layer(s))
                    n_gain += 1
                if n >= 2:
                    s2, i2 = w_order[n - 2]
                    name2 = W_BLOCKS[layer(s2)][i2][0]
                    sp.wait_ge(acc_done.sem, acc_done.count(s2, last_use.get(name2, name2)))
                sp.dma_start(wbuf[:, n % 2, 0:size], wts[W_BASE[layer(s)] + i, :, 0:size]).then_inc(w_in[n % 2], 16)
                if name == "out1":
                    load_gain(n_gain, 2 * layer(s) + 1)
                    n_gain += 1
                if name in ("q0", "q1", "q2", "q3"):
                    b = int(name[1])
                    m = 4 * s + b
                    if m >= 2:
                        sp.wait_ge(sc_done.sem, sc_done.count((m - 2) // 4, f"key{(m - 2) % 4}"))
                    sp.dma_start(kbuf[:, m % 2, :], keys[layer(s), b]).then_inc(k_in[m % 2], 16)
            load_gain(n_gain, 6)
            for t in range(TILES):
                s = (LAYERS - 1) * TILES + t
                sp.wait_ge(out_ready.sem, out_ready.count(s, "final"))
                sp.dma_start(out[t * P:(t + 1) * P, :], h[:, t, :]).then_inc(stored, 16)
            sp.wait_ge(stored, 16 * TILES)

        @block.gpsimd
        def _(pool):
            for kind, s, g in SCHEDULE:
                if kind != "G":
                    continue
                if g % PAIR == 0:
                    pool.wait_ge(idx_ready.sem, idx_ready.count(s, g // PAIR))
                for k in range(g * GROUP, (g + 1) * GROUP):
                    n = s * SLOTS + k
                    if n >= RING:
                        slot_done(pool, n - RING)
                    nc.gpsimd.indirect_dma_start(
                        ring[:, n % RING, :], None, uv[layer(s)],
                        bass.IndirectOffsetOnAxis(ap=idx[:, tile(s), k:k + 1], axis=0),
                    ).then_inc(row_in[n % RING], 16)

        @block.tensor
        def _(pe):
            def acc_free(s, name):
                n = acc_index[s, name]
                if n >= 2:
                    s2, name2, e = acc_order[n - 2]
                    pe.wait_ge(acc_out[e].sem, acc_out[e].count(s2, name2))

            def tp_free(s, name):
                n = tp_index[s, name]
                if n >= 2:
                    pe.wait_ge(tp_copied.sem, n - 1)

            def sc_free(s, name):
                n = sc_index[s, name]
                if n >= 2:
                    pe.wait_ge(sc_read.sem, n - 1)

            def weights(s, name):
                n = w_index[s, name]
                pe.wait_ge(w_in[n % 2], 16 * (n // 2 + 1))
                return wbuf[:, n % 2, :]

            def product(s, name, wname, cols=BLK, kts=range(KT), width=BLK, off=0, base=0):
                acc_free(s, name)
                w = weights(s, wname)
                for i, k in enumerate(kts):
                    mm = nc.tensor.matmul(acc_bank(s, name)[:, 0:cols], fT[:, k, :],
                                          w[:, base + i * width + off:base + i * width + off + cols],
                                          start=(i == 0), stop=(i == len(kts) - 1))
                mm.then_inc(acc_done.sem, 1)

            def product_T(s, name, wname):
                acc_free(s, name)
                w = weights(s, wname).rearrange("p (k n) -> p k n", k=KT)
                for j in range(4):
                    for k in range(KT):
                        mm = nc.tensor.matmul(acc_bank(s, name)[:, j * P:(j + 1) * P], w[:, k, j * P:(j + 1) * P],
                                              fT[:, k, :], start=(k == 0), stop=(k == KT - 1))
                mm.then_inc(acc_done.sem, 1)

            def turn(s, name, sources, rows=P):
                tp_free(s, name)
                for j, src in enumerate(sources):
                    mm = nc.tensor.transpose(tp_bank(s, name)[0:rows, j * P:(j + 1) * P], src, id_s[:])
                mm.then_inc(tp_done.sem, 1)

            def turn_rows(s, names, src):
                for i, name in enumerate(names):
                    turn(s, name, [src[:, (4 * i + j) * P:(4 * i + j + 1) * P] for j in range(4)])

            def scores(s, part, c):
                name = f"{part}_s{c}"
                sc_free(s, name)
                hg, kl = heads_per_chunk(s), keys_len(s)
                bank = sc_bank(s, name)
                hs = chunk_heads(s, part, c)
                for i, hd in enumerate(range(hs.start, hs.stop, hs.step)):
                    if part == "win":
                        b = hd % 2
                        lhs, rhs = qT[64 * b:64 * b + 64, hd // 2, :], c0_kT[64 * b:64 * b + 64, hd // 8, 0:kl]
                    elif part == "moba":
                        b = hd % 2
                        lhs, rhs = qT[64 * b:64 * b + 64, hd // 2, :], c2_kaT[64 * b:64 * b + 64, hd // 2, 0:kl]
                    else:
                        lhs, rhs = qT[0:96, hd, :], c2_kbT[0:96, hd, 0:kl]
                    mm = nc.tensor.matmul(bank[:, i * kl:(i + 1) * kl], lhs, rhs, start=True, stop=True)
                mm.then_inc(sc_done.sem, 1)

            def weigh(s, part, c):
                name = f"{part}_s{c}"
                hg, nk = heads_per_chunk(s), tile(s) + 1
                m = at_index[s, name]
                pe.wait_ge(probs.sem, probs.count(s, name))
                turn(s, f"{part}_p{c}", [sm[:, m % 2, j * P:(j + 1) * P] for j in range(4)])
                per_bank = 8
                hs = chunk_heads(s, part, c)
                o = f"o_{part}{hs.start // per_bank}"
                if c % (per_bank // hg) == 0:
                    acc_free(s, o)
                pe.wait_ge(tp_copied.sem, tp_copied.count(s, f"{part}_p{c}"))
                for i, hd in enumerate(range(hs.start, hs.stop, hs.step)):
                    for kt in range(nk):
                        if part == "win":
                            g = 2 * (hd // 8) + hd % 2
                            v = c0_v[:, kt, 64 * g:64 * g + 64]
                        else:
                            v = (c2_va if part == "moba" else c2_vb)[:, kt, 64 * hd:64 * hd + 64]
                        mm = nc.tensor.matmul(acc_bank(s, o)[:, (hd % per_bank) * 64:(hd % per_bank) * 64 + 64],
                                              pT[:, m % 2, (i * nk + kt) * P:(i * nk + kt + 1) * P], v,
                                              start=(kt == 0), stop=(kt == nk - 1))
                if (c + 1) % (per_bank // hg) == 0:
                    mm.then_inc(acc_done.sem, 1)

            def dense(s, p):
                l = layer(s)
                if p == "mix_T":
                    if s == 0:
                        pe.wait_ge(const_in, 16 * N_CONST)
                    pe.wait_ge(h_ready.sem, h_ready.count(s, "mix"))
                    turn_rows(s, ["mix0", "mix1"], h[:, tile(s), :])
                elif p == "ffn_T":
                    pe.wait_ge(h_ready.sem, h_ready.count(s, "ffn"))
                    turn_rows(s, ["ffn0", "ffn1"], h[:, tile(s), :])
                elif p.startswith("query"):
                    b = int(p[5:])
                    if b < 4:
                        if b == 0:
                            pe.wait_ge(tp_copied.sem, tp_copied.count(s, "ffn1"))
                        product_T(s, f"q{b}", f"q{b}")
                    if b > 0:
                        b -= 1
                        name = f"key{b}"
                        m = 4 * s + b
                        sc_free(s, name)
                        pe.wait_ge(k_in[m % 2], 16 * (m // 2 + 1))
                        pe.wait_ge(acc_out["act"].sem, acc_out["act"].count(s, f"q{b}"))
                        for j in range(4):
                            mm = nc.tensor.matmul(sc_bank(s, name)[:, j * P:(j + 1) * P],
                                                  queryT[:, m % 2, j * P:(j + 1) * P],
                                                  kbuf[:, m % 2, j * P:(j + 1) * P], start=True, stop=True)
                        mm.then_inc(sc_done.sem, 1)
                elif p in ("qkv0", "qkv1", "qkv2") or (l == 2 and p in ("q", "k", "v", "lat", "ga0", "ga1", "gb0", "gb1")):
                    if p in ("qkv0", "q"):
                        pe.wait_ge(tp_copied.sem, tp_copied.count(s, "mix1"))
                    if p == "lat":
                        product(s, p, p, cols=416, width=416)
                    else:
                        product(s, p, p)
                elif l == 1 and p in ("c0", "u0", "c1", "u1", "b0", "b1"):
                    if p == "c0":
                        pe.wait_ge(tp_copied.sem, tp_copied.count(s, "mix1"))
                    product_T(s, p, p)
                elif p == "qk_T":
                    pe.wait_ge(dve_at.sem, dve_at.count(s, "qk_norm"))
                    for i in range(2):
                        turn(s, f"win_q{i}", [big[:, (4 * i + j) * P:(4 * i + j + 1) * P] for j in range(4)])
                    turn(s, "win_k", [big[:, 1024 + j * P:1024 + (j + 1) * P] for j in range(2)])
                elif p == "moba_T":
                    pe.wait_ge(dve_at.sem, dve_at.count(s, "moba_rope"))
                    turn(s, "moba_q", [qk[:, j * P:(j + 1) * P] for j in range(4)])
                    turn(s, "moba_k", [qk[:, 512 + j * P:512 + (j + 1) * P] for j in range(4)])
                elif p == "lat_T":
                    pe.wait_ge(dve_at.sem, dve_at.count(s, "lat_norm"))
                    turn(s, "lat", [lat[:, j * P:(j + 1) * P] for j in range(3)])
                elif p in ("uq0", "uq1", "uk", "uv"):
                    if p == "uq0":
                        pe.wait_ge(tp_copied.sem, tp_copied.count(s, "lat"))
                    if p == "uq0":
                        product(s, p, "ups", kts=range(2), width=768)
                    elif p == "uq1":
                        product(s, p, "ups", cols=256, kts=range(2), width=768, off=512)
                    else:
                        product(s, p, "ups", kts=[2], base=2 * 768, off=512 * (p == "uv"))
                elif p == "mla_T":
                    pe.wait_ge(dve_at.sem, dve_at.count(s, "mla_rope"))
                    for i in range(2):
                        turn(s, f"mla_q{i}", [qk[:, (4 * i + j) * 96:(4 * i + j + 1) * 96] for j in range(4)], rows=96)
                    for i in range(2):
                        turn(s, f"mla_k{i}", [kfull[:, 4 * i + j, :] for j in range(4)], rows=96)
                elif "_chunk" in p:
                    part, c = p.split("_chunk")
                    c = int(c)
                    if c == 0:
                        last = {"win": "win_k", "moba": "moba_k", "mla": "mla_k1"}[part]
                        pe.wait_ge(tp_copied.sem, tp_copied.count(s, last))
                    if c < chunks(s, part):
                        scores(s, part, c)
                    if c > 0:
                        weigh(s, part, c - 1)
                elif p == "win_oT":
                    pe.wait_ge(acc_out["dve"].sem, acc_out["dve"].count(s, "o_win1"))
                    turn_rows(s, ["win_o0", "win_o1"], oM)
                elif p == "oT":
                    pe.wait_ge(acc_out["dve"].sem, acc_out["dve"].count(s, "o_mla0"))
                    turn_rows(s, ["o0", "o1"], oM)
                elif p in ("br0", "br1"):
                    n = int(p[2])
                    if n == 0:
                        pe.wait_ge(tp_copied.sem, tp_copied.count(s, "o1"))
                        weights(s, "bra")
                        weights(s, "brb")
                    for e, kts in (("bra", range(4)), ("brb", range(4, 8))):
                        product(s, f"{e}{n}", e, kts=kts, width=D, off=BLK * n)
                elif p == "mrg_T":
                    pe.wait_ge(dve_at.sem, dve_at.count(s, "mrg"))
                    turn_rows(s, ["mrg0", "mrg1"], oM)
                elif p in ("out0", "out1"):
                    if p == "out0":
                        if l == 1:
                            pe.wait_ge(acc_out["dve"].sem, acc_out["dve"].count(s, "b1"))
                        else:
                            pe.wait_ge(tp_copied.sem, tp_copied.count(s, "win_o1" if l == 0 else "mrg1"))
                    product(s, p, p)

            for kind, s, p in SCHEDULE:
                if kind == "D":
                    dense(s, p)
                elif kind == "G":
                    if p == 0 and s > 0:
                        pe.wait_ge(x_moved.sem, x_moved.count(s - 1, "y"))
                    for k in range(p * GROUP, (p + 1) * GROUP):
                        if k % TURN in BY_VECTOR:
                            continue
                        n = s * SLOTS + k
                        d = diags.count(s, k)
                        pe.wait_ge(diags.sem, d)
                        for half in range(2):
                            mm = nc.tensor.matmul(y[half][:], diag[:, (d - 1) % DIAGS, :],
                                                  ring[:, n % RING, D + half * BLK:D + (half + 1) * BLK],
                                                  start=(k == by_tensor[0]), stop=(k == by_tensor[-1]))
                        mm.then_inc(y_slot.sem, 1)

        @block.scalar
        def _(act):
            n_act = [0]

            def mark(ins):
                n_act[0] += 1
                return ins.then_inc(act_step, 1)

            def settle():
                act.wait_ge(act_step, n_act[0])

            def copy(dst, src):
                return nc.scalar.activation(dst, src, ACT.Copy)

            def from_acc(s, name, dst, cols=BLK, func=ACT.Copy):
                act.wait_ge(acc_done.sem, acc_done.count(s, name))
                nc.scalar.activation(dst, acc_bank(s, name)[:, 0:cols], func).then_inc(acc_out["act"].sem, 1)

            def from_tp(s, name, dst, rows=P, cols=BLK):
                act.wait_ge(tp_done.sem, tp_done.count(s, name))
                src = tp_bank(s, name)[0:rows, 0:cols]
                if len(dst.shape) == 3:
                    src = src.rearrange("p (a n) -> p a n", a=dst.shape[1])
                copy(dst, src).then_inc(tp_copied.sem, 1)

            def root_mean_square(s, which):
                if which == "mix":
                    if s < TILES:
                        act.wait_ge(x_in, 16 * TILES)
                    else:
                        act.wait_ge(x_moved.sem, x_moved.count(s - 2, "y"))
                elif which == "ffn":
                    act.wait_ge(acc_out["dve"].sem, acc_out["dve"].count(s, "out1"))
                else:
                    act.wait_ge(x_moved.sem, x_moved.count(s, "y"))
                mark(nc.scalar.activation(oM[:, 0:D], x[:, tile(s), :], ACT.Square, accum_out=st[:, 0:1]))
                settle()
                nc.scalar.activation(st[:, 1:2], st[:, 0:1], ACT.Sqrt, scale=1.0 / D,
                                     bias=epsc[:]).then_inc((last_sq if which == "final" else sq_ready).sem, 1)

            def dense(s, p):
                l, t = layer(s), tile(s)
                if p == "mix_stat":
                    root_mean_square(s, "mix")
                elif p == "ffn_stat":
                    root_mean_square(s, "ffn")
                elif p == "mix_T":
                    for i in range(2):
                        from_tp(s, f"mix{i}", fT[:, 4 * i:4 * i + 4, :])
                elif p == "ffn_T":
                    for i in range(2):
                        from_tp(s, f"ffn{i}", fT[:, 4 * i:4 * i + 4, :])
                elif p.startswith("query") and p != "query4":
                    b = int(p[5:])
                    m = 4 * s + b
                    if m >= 2:
                        act.wait_ge(sc_done.sem, sc_done.count((m - 2) // 4, f"key{(m - 2) % 4}"))
                    from_acc(s, f"q{b}", queryT[:, m % 2, :])
                elif p.startswith("top"):
                    b = int(p[3:])
                    act.wait_ge(best_done.sem, best_done.count(s, b))
                    for i in range(2):
                        e = nc.scalar.activation(gate[:, t, (2 * b + i) * TOPK:(2 * b + i + 1) * TOPK], best[:, i, :],
                                                 ACT.Exp, bias=nbest[:, i:i + 1], accum_out=bsum[:, i:i + 1])
                    e.then_inc(gate_exp.sem, 1)
                elif p in ("qkv0", "qkv1"):
                    from_acc(s, p, big[:, 512 * int(p[3]):512 * int(p[3]) + 512])
                elif p == "qkv2":
                    act.wait_ge(acc_done.sem, acc_done.count(s, p))
                    mark(copy(big[:, 1024:1280], acc_bank(s, p)[:, 0:256]))
                    copy(c0_v[:, t, :], acc_bank(s, p)[:, 256:512]).then_inc(acc_out["act"].sem, 1)
                elif p == "qk_norm":
                    act.wait_ge(dve_at.sem, dve_at.count(s, "qk_sq"))
                    nc.scalar.activation(r20[:, 20:40], r20[:, 0:20], ACT.Sqrt, scale=1.0 / 64,
                                         bias=epsc[:]).then_inc(act_at.sem, 1)
                elif p == "qk_T":
                    for i in range(2):
                        from_tp(s, f"win_q{i}", qT[:, 4 * i:4 * i + 4, :])
                    from_tp(s, "win_k", c0_kT[:, :, t * P:(t + 1) * P], cols=256)
                elif p == "moba_T":
                    from_tp(s, "moba_q", qT[:, 0:4, :])
                    from_tp(s, "moba_k", c2_kaT[:, :, t * P:(t + 1) * P])
                elif p == "mla_T":
                    for i in range(2):
                        from_tp(s, f"mla_q{i}", qT[0:96, 4 * i:4 * i + 4, :], rows=96)
                    for i in range(2):
                        from_tp(s, f"mla_k{i}", c2_kbT[0:96, 4 * i:4 * i + 4, t * P:(t + 1) * P], rows=96)
                elif "_chunk" in p:
                    part, c = p.split("_chunk")
                    c = int(c)
                    if c > 0:
                        name = f"{part}_s{c - 1}"
                        from_tp(s, f"{part}_p{c - 1}", pT[:, at_index[s, name] % 2, :])
                    if c < chunks(s, part):
                        name = f"{part}_s{c}"
                        m = at_index[s, name] % 2
                        hg, kl = heads_per_chunk(s), keys_len(s)
                        act.wait_ge(max_done.sem, max_done.count(s, name))
                        hs = chunk_heads(s, part, c)
                        for i, hd in enumerate(range(hs.start, hs.stop, hs.step)):
                            e = nc.scalar.activation(sm[:, m, i * kl:(i + 1) * kl], sm[:, m, i * kl:(i + 1) * kl],
                                                     ACT.Exp, bias=nmx[:, hd:hd + 1], accum_out=den[:, hd:hd + 1])
                        e.then_inc(probs.sem, 1)
                elif p == "win_end":
                    act.wait_ge(dve_at.sem, dve_at.count(s, "win_den"))
                    nc.scalar.activation(esink[:], esink[:], ACT.Exp).then_inc(act_at.sem, 1)
                elif p in ("win_oT", "oT", "mrg_T"):
                    n = {"win_oT": "win_o", "oT": "o", "mrg_T": "mrg"}[p]
                    for i in range(2):
                        from_tp(s, f"{n}{i}", fT[:, 4 * i:4 * i + 4, :])
                elif l == 1 and p in ("c0", "c1"):
                    act.wait_ge(acc_done.sem, acc_done.count(s, p))
                    copy(big[:, 512 * int(p[1]):512 * int(p[1]) + 512], acc_bank(s, p)[:]).then_inc(acc_out["act"].sem, 1)
                elif l == 2 and p in ("q", "k"):
                    from_acc(s, p, qk[:, 512 * (p == "k"):512 * (p == "k") + 512])
                elif l == 2 and p == "v":
                    from_acc(s, p, c2_va[:, t, :])
                elif p == "lat":
                    from_acc(s, p, lat[:], cols=416)
                elif p in ("ga0", "ga1", "gb0", "gb1"):
                    o = D * (p[1] == "b") + BLK * int(p[2])
                    from_acc(s, p, big[:, o:o + BLK], func=ACT.Sigmoid)
                elif p == "lat_norm":
                    act.wait_ge(dve_at.sem, dve_at.count(s, "lat_sq"))
                    mark(nc.scalar.activation(st[:, 6:7], st[:, 4:5], ACT.Sqrt, scale=1.0 / 256, bias=epsc[:]))
                    nc.scalar.activation(st[:, 7:8], st[:, 5:6], ACT.Sqrt, scale=1.0 / 128,
                                         bias=epsc[:]).then_inc(act_at.sem, 1)
                elif p == "lat_T":
                    from_tp(s, "lat", fT[:, 0:3, :], cols=3 * P)
                elif p in ("uq0", "uq1"):
                    from_acc(s, p, qk[:, 512 * int(p[2]):768 if p == "uq1" else 512], cols=256 if p == "uq1" else 512)
                elif p == "uk":
                    act.wait_ge(acc_done.sem, acc_done.count(s, p))
                    copy(kfull[:, :, 0:64], acc_bank(s, p)[:].rearrange("p (h n) -> p h n", h=8))\
                        .then_inc(acc_out["act"].sem, 1)
                elif p == "uv":
                    from_acc(s, p, c2_vb[:, t, :])

            act.wait_ge(trig_arg, 1)
            mark(nc.scalar.activation(sinr[:], ang[:], ACT.Sin))
            nc.scalar.activation(cosr[:], angk[:], ACT.Sin).then_inc(trig, 1)
            act.wait_ge(trig, 1)
            for kind, s, p in SCHEDULE:
                if kind == "D":
                    dense(s, p)
                elif kind == "G":
                    if p % PAIR == 0:
                        act.wait_ge(idx_ready.sem, idx_ready.count(s, p // PAIR))
                    k0 = p * GROUP
                    n0 = s * SLOTS + k0
                    c0 = n0 % ACOLS
                    act.wait_ge(dots.sem, dots.count(s, p))
                    mark(nc.scalar.activation(ge[:, c0:c0 + GROUP], a[:, c0:c0 + GROUP], ACT.Gelu))
                    settle()
                    for i in range(GROUP):
                        last = nc.scalar.activation(wgt[:, c0 + i:c0 + i + 1], ge[:, c0 + i:c0 + i + 1], ACT.Copy,
                                                    scale=gate[:, tile(s), k0 + i:k0 + i + 1])
                    last.then_inc(weights_at.sem, 1)
                    act.wait_ge(weights_at.sem, weights_at.count(s, p))
                    for i in range(GROUP):
                        if (k0 + i) % TURN in BY_VECTOR:
                            continue
                        d = diags.count(s, k0 + i)
                        if d > DIAGS:
                            act.wait_ge(y_slot.sem, d - DIAGS)
                        nc.scalar.activation(diag[:, (d - 1) % DIAGS, :], id_s[:], ACT.Copy,
                                             scale=wgt[:, c0 + i:c0 + i + 1]).then_inc(diags.sem, 1)
                elif kind == "X" and layer(s) == LAYERS - 1:
                    root_mean_square(s, "final")

        @block.vector
        def _(dve):
            n_dve = [0]
            n_norm = [0]
            v = nc.vector

            def mark(ins):
                n_dve[0] += 1
                return ins.then_inc(dve_step, 1)

            def settle():
                dve.wait_ge(dve_step, n_dve[0])

            def link(ins):
                mark(ins)
                settle()

            def norm(s, which):
                n_norm[0] += 1
                rms = last_sq if which == "final" else sq_ready
                dve.wait_ge(rms.sem, rms.count(s, which))
                link(v.reciprocal(st[:, 2:3], st[:, 1:2]))
                dve.wait_ge(gain_in, 16 * (n_norm[0] if which != "final" else 2 * STEPS + 1))
                ins = v.scalar_tensor_tensor(h[:, tile(s), :], x[:, tile(s), :], st[:, 2:3], gain[:], ALU.mult, ALU.mult)
                return ins

            def rope(x1, x2, o1, o2, cos, sin, n, w, scratch):
                t1, t2, t3, t4 = [scratch[:, i * n * w:(i + 1) * n * w].rearrange("p (h n) -> p h n", h=n) for i in range(4)]
                cb, sb_ = cos.unsqueeze(1).broadcast_to([P, n, w]), sin.unsqueeze(1).broadcast_to([P, n, w])
                mark(v.tensor_tensor(t1, x1, cb, ALU.mult))
                mark(v.tensor_tensor(t2, x2, sb_, ALU.mult))
                mark(v.tensor_tensor(t3, x2, cb, ALU.mult))
                mark(v.tensor_tensor(t4, x1, sb_, ALU.mult))
                settle()
                mark(v.tensor_tensor(o1, t1, t2, ALU.subtract))
                return v.tensor_tensor(o2, t3, t4, ALU.add)

            def softmax_chunk(s, part, c):
                name = f"{part}_s{c}"
                hg, kl = heads_per_chunk(s), keys_len(s)
                m = at_index[s, name]
                dve.wait_ge(sc_done.sem, sc_done.count(s, name))
                if m >= 2:
                    s2, name2 = at_order[m - 2]
                    dve.wait_ge(tp_done.sem, tp_done.count(s2, name2.replace("_s", "_p")))
                if tile(s) == 0:
                    mk = mask_s[:, 1, :]
                else:
                    mk = (mask_s[:, 0:2, :] if part == "win" else mask_s[:, 2:4, :]).rearrange("p a n -> p (a n)")
                smv = sm[:, m % 2, :].rearrange("p (h n) -> p h n", h=hg)
                v.scalar_tensor_tensor(smv, sc_bank(s, name)[:].rearrange("p (h n) -> p h n", h=hg), SCALE[part],
                                       mk.unsqueeze(1).broadcast_to([P, hg, kl]), ALU.mult, ALU.add)\
                    .then_inc(sc_read.sem, 1)
                dve.wait_ge(sc_read.sem, sc_read.count(s, name))
                hs = chunk_heads(s, part, c)
                link(v.tensor_reduce(mx[:, hs], smv, AXX, ALU.max))
                if part == "win":
                    link(v.tensor_tensor(mx[:, hs], mx[:, hs], sink[:, hs], ALU.max))
                v.tensor_scalar(nmx[:, hs], mx[:, hs], -1.0, None, ALU.mult).then_inc(max_done.sem, 1)

            def out_of_attention(s, part, col):
                n = HEADS[part]
                link(v.reciprocal(rden[:, 0:n], den[:, 0:n]))
                for half in range(n // 8):
                    o = f"o_{part}{half}"
                    dve.wait_ge(acc_done.sem, acc_done.count(s, o))
                    v.tensor_tensor(oM[:, col + half * BLK:col + (half + 1) * BLK].rearrange("p (h n) -> p h n", h=8),
                                    acc_bank(s, o)[:].rearrange("p (h n) -> p h n", h=8),
                                    rden[:, half * 8:half * 8 + 8].unsqueeze(2).broadcast_to([P, 8, 64]), ALU.mult)\
                        .then_inc(acc_out["dve"].sem, 1)

            def choose(s, b):
                t = tile(s)
                name = f"key{b}"
                dve.wait_ge(sc_done.sem, sc_done.count(s, name))
                keys_of = [sc_bank(s, name)[:, j * P:(j + 1) * P] for j in range(4)]
                rest_of = [swork[:, j * P:(j + 1) * P] for j in range(4)]
                for j in range(4):
                    mark(v.max(tv[:, j, 0:8], keys_of[j]))
                settle()
                for j in range(4):
                    mark(v.max_index(ti[:, j, 0:8], tv[:, j, 0:8], keys_of[j]))
                for j in range(4):
                    ins = v.match_replace(rest_of[j], tv[:, j, 0:8], keys_of[j], -3e38)
                ins.then_inc(sc_read.sem, 1)
                dve.wait_ge(sc_read.sem, sc_read.count(s, name))
                for j in range(4):
                    mark(v.max(tv[:, j, 8:16], rest_of[j]))
                settle()
                for j in range(4):
                    mark(v.max_index(ti[:, j, 8:16], tv[:, j, 8:16], rest_of[j]))
                for i in range(2):
                    mark(v.tensor_tensor(cand[:, i, :].rearrange("p (a b) -> p a b", a=TOPK),
                                         tv[:, 2 * i, :].unsqueeze(2).broadcast_to([P, TOPK, TOPK]),
                                         tv[:, 2 * i + 1, :].unsqueeze(1).broadcast_to([P, TOPK, TOPK]), ALU.add))
                settle()
                mark(v.tensor_copy(tf[:], ti[:]))
                rest2 = [hot[:, i, 0:TOPK, :].rearrange("p a b -> p (a b)") for i in range(2)]
                for i in range(2):
                    mark(v.max(best[:, i, 0:8], cand[:, i, :]))
                settle()
                for i in range(2):
                    mark(v.max_index(posu[:, i, 0:8], best[:, i, 0:8], cand[:, i, :]))
                    mark(v.match_replace(rest2[i], best[:, i, 0:8], cand[:, i, :], -3e38))
                v.tensor_scalar(nbest[:], best[:, :, 0], -1.0, None, ALU.mult)
                settle()
                for i in range(2):
                    ins = v.max(best[:, i, 8:16], rest2[i])
                ins.then_inc(best_done.sem, 1)
                dve.wait_ge(best_done.sem, best_done.count(s, b))
                for i in range(2):
                    mark(v.max_index(posu[:, i, 8:16], best[:, i, 8:16], rest2[i]))
                settle()
                link(v.tensor_scalar(posu[:, :, TOPK:], posu[:, :, 0:TOPK], 15, None, ALU.bitwise_and))
                link(v.tensor_scalar(posu[:, :, 0:TOPK], posu[:, :, 0:TOPK], 4, None, ALU.logical_shift_right))
                link(v.tensor_copy(posn[:], posu[:]))
                link(v.tensor_tensor(hot[:].rearrange("p a b c -> p (a b) c"),
                                     posn[:].rearrange("p a b -> p (a b)").unsqueeze(2).broadcast_to([P, 4 * TOPK, TOPK]),
                                     iota_s[:].unsqueeze(1).broadcast_to([P, 4 * TOPK, TOPK]), ALU.is_equal))
                hot4 = hot[:].rearrange("p a (u b) c -> p (a u) b c", u=2)
                link(v.tensor_tensor(hot4, hot4, tf[:].unsqueeze(2).broadcast_to([P, 4, TOPK, TOPK]), ALU.mult))
                link(v.tensor_reduce(isel[:].rearrange("p a b -> p (a b)"), hot[:].rearrange("p a b c -> p (a b) c"),
                                     AXX, ALU.add))
                cols = slice(2 * b * TOPK, (2 * b + 2) * TOPK)
                mark(v.scalar_tensor_tensor(idx[:, t, cols].rearrange("p (a b) -> p a b", a=2), isel[:, :, 0:TOPK],
                                            float(N_KEYS), isel[:, :, TOPK:], ALU.mult, ALU.add))
                dve.wait_ge(gate_exp.sem, gate_exp.count(s, b))
                link(v.reciprocal(bsum[:], bsum[:]))
                gv = gate[:, t, cols].rearrange("p (a b) -> p a b", a=2)
                v.tensor_tensor(gv, gv, bsum[:].unsqueeze(2).broadcast_to([P, 2, TOPK]), ALU.mult)\
                    .then_inc(idx_ready.sem, 1)

            def add_rows(s, g):
                mine = [k for k in range(g * GROUP, (g + 1) * GROUP) if k in by_vector]
                if mine:
                    dve.wait_ge(weights_at.sem, weights_at.count(s, g))
                for k in mine:
                    n = s * SLOTS + k
                    m = x_slot.count(s, k)
                    if m > 1:
                        dve.wait_ge(x_slot.sem, m - 1)
                    xs = x[:, tile(s), :]
                    v.scalar_tensor_tensor(xs, ring[:, n % RING, D:2 * D], wgt[:, n % ACOLS:n % ACOLS + 1], xs,
                                           ALU.mult, ALU.add).then_inc(x_slot.sem, 1)

            def add_to_x(s, half, name):
                dve.wait_ge(acc_done.sem, acc_done.count(s, name))
                xs = x[:, tile(s), half * BLK:(half + 1) * BLK]
                v.tensor_tensor(xs, xs, acc_bank(s, name)[:], ALU.add).then_inc(acc_out["dve"].sem, 1)

            def dense(s, p):
                l, t = layer(s), tile(s)
                if p == "mix_stat":
                    norm(s, "mix").then_inc(h_ready.sem, 1)
                elif p == "ffn_stat":
                    norm(s, "ffn").then_inc(h_ready.sem, 1)
                elif p.startswith("top"):
                    choose(s, int(p[3:]))
                elif p in ("out0", "out1"):
                    add_to_x(s, int(p[3]), p)
                elif p == "qk_norm":
                    n = 20
                    dve.wait_ge(acc_out["act"].sem, acc_out["act"].count(s, "qkv2"))
                    qkv = big[:, 0:1280].rearrange("p (h n) -> p h n", h=n)
                    sq = qk[:, 0:1280].rearrange("p (h n) -> p h n", h=n)
                    link(v.tensor_tensor(sq, qkv, qkv, ALU.mult))
                    v.tensor_reduce(r20[:, 0:20], sq, AXX, ALU.add).then_inc(dve_at.sem, 1)
                    dve.wait_ge(act_at.sem, act_at.count(s, "qk_rms"))
                    link(v.reciprocal(r20[:, 0:20], r20[:, 20:40]))
                    link(v.tensor_tensor(qkv, qkv, r20[:, 0:20].unsqueeze(2).broadcast_to([P, n, 64]), ALU.mult))
                    for heads, g0 in ((slice(0, 16), 0), (slice(16, 20), 64)):
                        m = heads.stop - heads.start
                        mark(v.tensor_tensor(qkv[:, heads, :], qkv[:, heads, :],
                                             smallr[:, g0:g0 + 64].unsqueeze(1).broadcast_to([P, m, 64]), ALU.mult))
                    settle()
                    rope(qkv[:, :, 0:8], qkv[:, :, 8:16], qkv[:, :, 0:8], qkv[:, :, 8:16],
                         rc[:, t, 0:8], rc[:, t, 8:16], n, 8, qk).then_inc(dve_at.sem, 1)
                elif "_chunk" in p:
                    part, c = p.split("_chunk")
                    if int(c) < chunks(s, part):
                        softmax_chunk(s, part, int(c))
                elif p == "win_end":
                    dve.wait_ge(max_done.sem, max_done.count(s, f"win_s{chunks(s, 'win') - 1}"))
                    v.tensor_tensor(esink[:], nmx[:], sink[:], ALU.add).then_inc(dve_at.sem, 1)
                    dve.wait_ge(act_at.sem, act_at.count(s, "win_esink"))
                    link(v.tensor_tensor(den[:], den[:], esink[:], ALU.add))
                    out_of_attention(s, "win", 0)
                elif p == "moba_end":
                    dve.wait_ge(probs.sem, probs.count(s, f"moba_s{chunks(s, 'moba') - 1}"))
                    out_of_attention(s, "moba", 0)
                elif p == "mla_end":
                    dve.wait_ge(probs.sem, probs.count(s, f"mla_s{chunks(s, 'mla') - 1}"))
                    out_of_attention(s, "mla", 512)
                elif l == 1 and p in ("u0", "u1"):
                    j = int(p[1])
                    z4 = z[:, 4 * j:4 * j + 4, :]
                    if t == 0:
                        mark(v.memset(z4[:, :, 0:2], 0.0))
                    else:
                        mark(v.tensor_copy(z4[:, :, 0:2], z4[:, :, P:P + 2]))
                        settle()
                    dve.wait_ge(acc_out["act"].sem, acc_out["act"].count(s, f"c{j}"))
                    dve.wait_ge(acc_done.sem, acc_done.count(s, p))
                    v.tensor_tensor(z4[:, :, 2:P + 2], acc_bank(s, p)[:].rearrange("p (c n) -> p c n", c=4),
                                    big[:, 512 * j:512 * j + 512].rearrange("p (c n) -> p c n", c=4), ALU.mult)\
                        .then_inc(acc_out["dve"].sem, 1)
                    dve.wait_ge(acc_out["dve"].sem, acc_out["dve"].count(s, p))
                    settle()
                    cv = big[:, D + 512 * j:D + 512 * j + 512].rearrange("p (c n) -> p c n", c=4)
                    tv4 = tmp[:, 0:512].rearrange("p (c n) -> p c n", c=4)
                    for i in range(3):
                        link(v.tensor_tensor(tv4 if i else cv, z4[:, :, i:i + P],
                                             cw[:, 4 * j:4 * j + 4, i].unsqueeze(2).broadcast_to([P, 4, P]), ALU.mult))
                        if i:
                            link(v.tensor_tensor(cv, cv, tv4, ALU.add))
                elif l == 1 and p == "b1":
                    dve.wait_ge(acc_done.sem, acc_done.count(s, "b1"))
                    for j in range(2):
                        v.tensor_tensor(fT[:, 4 * j:4 * j + 4, :].rearrange("p c n -> p (c n)"), acc_bank(s, f"b{j}")[:],
                                        big[:, D + 512 * j:D + 512 * j + 512], ALU.mult).then_inc(acc_out["dve"].sem, 1)
                elif p == "moba_rope":
                    dve.wait_ge(acc_out["act"].sem, acc_out["act"].count(s, "k"))
                    dve.wait_ge(trig, 1)
                    dve.wait_ge(dve_at.sem, dve_at.count(s, "lat_sq"))
                    q3 = qk[:, 0:1024].rearrange("p (h n) -> p h n", h=16)
                    for i in range(2):
                        hs = slice(8 * i, 8 * i + 8)
                        last = rope(q3[:, hs, 0:32], q3[:, hs, 32:64], q3[:, hs, 0:32], q3[:, hs, 32:64],
                                    cosr[:, t, 0:32], sinr[:, t, 0:32], 8, 32, tmp)
                        if i == 0:
                            link(last)
                    last.then_inc(dve_at.sem, 1)
                elif p == "lat":
                    dve.wait_ge(acc_out["act"].sem, acc_out["act"].count(s, "lat"))
                    mark(v.tensor_tensor_reduce(tmp[:, 0:256], lat[:, 0:256], lat[:, 0:256], 1.0, 0.0, ALU.mult, ALU.add,
                                                st[:, 4:5]))
                    v.tensor_tensor_reduce(tmp[:, 256:384], lat[:, 256:384], lat[:, 256:384], 1.0, 0.0, ALU.mult,
                                           ALU.add, st[:, 5:6]).then_inc(dve_at.sem, 1)
                elif p == "lat_norm":
                    dve.wait_ge(act_at.sem, act_at.count(s, "lat_rms"))
                    link(v.reciprocal(st[:, 8:10], st[:, 6:8]))
                    mark(v.scalar_tensor_tensor(lat[:, 0:256], lat[:, 0:256], st[:, 8:9], smallr[:, 128:384],
                                                ALU.mult, ALU.mult))
                    v.scalar_tensor_tensor(lat[:, 256:384], lat[:, 256:384], st[:, 9:10], smallr[:, 384:512],
                                           ALU.mult, ALU.mult).then_inc(dve_at.sem, 1)
                elif p == "mla_rope":
                    cb, sb_ = cosr[:, t, 32:48], sinr[:, t, 32:48]
                    l3 = lat[:, 384:416].unsqueeze(1)
                    scratch = tmp[:, 768:1280]
                    dve.wait_ge(acc_out["act"].sem, acc_out["act"].count(s, "uk"))
                    link(rope(l3[:, :, 0:16], l3[:, :, 16:32], l3[:, :, 0:16], l3[:, :, 16:32], cb, sb_, 1, 16, scratch))
                    mark(v.tensor_copy(kfull[:, :, 64:96], lat[:, 384:416].unsqueeze(1).broadcast_to([P, 8, 32])))
                    q3 = qk[:, 0:768].rearrange("p (h n) -> p h n", h=8)
                    rope(q3[:, :, 64:80], q3[:, :, 80:96], q3[:, :, 64:80], q3[:, :, 80:96], cb, sb_, 8, 16, scratch)\
                        .then_inc(dve_at.sem, 1)
                elif p in ("br0", "br1"):
                    n = int(p[2])
                    dst = oM[:, n * BLK:(n + 1) * BLK]
                    dve.wait_ge(acc_done.sem, acc_done.count(s, f"bra{n}"))
                    v.tensor_tensor(dst, acc_bank(s, f"bra{n}")[:], big[:, n * BLK:(n + 1) * BLK], ALU.mult)\
                        .then_inc(acc_out["dve"].sem, 1)
                    dve.wait_ge(acc_done.sem, acc_done.count(s, f"brb{n}"))
                    v.tensor_tensor(tmp[:, 0:BLK], acc_bank(s, f"brb{n}")[:], big[:, D + n * BLK:D + (n + 1) * BLK],
                                    ALU.mult).then_inc(acc_out["dve"].sem, 1)
                    dve.wait_ge(acc_out["dve"].sem, acc_out["dve"].count(s, f"brb{n}"))
                    last = v.tensor_tensor(dst, dst, tmp[:, 0:BLK], ALU.add)
                    if n == 0:
                        link(last)
                    else:
                        last.then_inc(dve_at.sem, 1)

            link(v.memset(epsc[:], EPS))
            dve.wait_ge(const_in, 16 * N_CONST)
            link(v.tensor_copy(posf[:], posi[:]))
            for t in range(TILES):
                mark(v.tensor_scalar(ang[:, t, :], inv[:], posf[:, t:t + 1], None, ALU.mult))
            settle()
            link(v.tensor_scalar(angk[:], ang[:], 1.0 / TWO_PI, ROUND, ALU.mult, ALU.add))
            link(v.tensor_scalar(angk[:], angk[:], -ROUND, None, ALU.add))
            for c in (C1, C2, C3):
                link(v.scalar_tensor_tensor(ang[:], angk[:], -c, ang[:], ALU.mult, ALU.add))
            link(v.tensor_scalar(ang[:], ang[:], PI, -PI, ALU.min, ALU.max))
            link(v.scalar_tensor_tensor(angk[:], ang[:], -1.0, ang[:], ALU.mult, ALU.max))
            v.tensor_scalar(angk[:], angk[:], -1.0, PI / 2, ALU.mult, ALU.add).then_inc(trig_arg, 1)
            dve.wait_ge(x_in, 16 * TILES)

            for kind, s, p in SCHEDULE:
                if kind == "D":
                    dense(s, p)
                elif kind == "G":
                    for k in range(p * GROUP, (p + 1) * GROUP):
                        n = s * SLOTS + k
                        c = n % ACOLS
                        dve.wait_ge(row_in[n % RING], 16 * (n // RING + 1))
                        u = ring[:, n % RING, 0:D]
                        ins = v.tensor_tensor_reduce(u, u, h[:, tile(s), :], 1.0, 0.0, ALU.mult, ALU.add, a[:, c:c + 1])
                    ins.then_inc(dots.sem, 1)
                    if p > 0:
                        add_rows(s, p - 1)
                else:
                    add_rows(s, GROUPS - 1)
                    dve.wait_ge(x_slot.sem, x_slot.count(s, by_vector[-1]))
                    dve.wait_ge(y_slot.sem, y_slot.count(s, by_tensor[-1]))
                    for half in range(2):
                        xs = x[:, tile(s), half * BLK:(half + 1) * BLK]
                        last = v.tensor_tensor(xs, xs, y[half][:], ALU.add)
                    last.then_inc(x_moved.sem, 1)
                    if layer(s) == LAYERS - 1:
                        norm(s, "final").then_inc(out_ready.sem, 1)


def kernel(**inputs):
    import concourse.bacc as bacc
    from concourse.bass_utils import run_bass_kernel_spmd

    f = {k: np.asarray(v) for k, v in inputs.items()}

    def block(w):
        k, n = w.shape
        flat = w.reshape(k // P, P, n).transpose(1, 0, 2).reshape(P, -1)
        return flat

    def padded(blocks):
        out = np.zeros((len(blocks), P, WBLK), np.float32)
        for i, b in enumerate(blocks):
            out[i, :, :b.shape[1]] = b
        return out

    def columns(w):
        return [block(w[:, i:i + BLK]) for i in range(0, w.shape[1], BLK)]

    order = np.arange(16).reshape(2, 2, 4).transpose(0, 2, 1).reshape(-1)
    w_qkv, w_o = f["attn_w_qkv"][0], f["attn_w_o"][0]
    w_q = w_qkv[:, :D].reshape(D, 16, 64)[:, order].reshape(D, D)
    w_o = w_o.reshape(16, 64, D)[order].reshape(D, D)
    win = f["w_in_2"][0]
    kv_up = f["w_kv_up_2"][0].reshape(P, 8, 2, 64).transpose(0, 2, 1, 3).reshape(P, D)
    cin = f["conv_w_in"][0]
    queries = [f["peer_w_query"][0], f["peer_w_query"][1], f["w_peer_query_2"][0]]
    mixers = [
        columns(w_q) + columns(w_qkv[:, D:]) + columns(w_o),
        columns(np.concatenate([cin[:, D:D + BLK], cin[:, 2 * D:2 * D + BLK], cin[:, D + BLK:2 * D],
                                cin[:, 2 * D + BLK:], cin[:, :D]], axis=1)) + columns(f["conv_w_out"][0]),
        columns(win[:, :1536]) + [block(win[:, 1536:1952])] + columns(win[:, 1952:])
        + [np.concatenate([block(f["w_q_up_2"][0]), kv_up], axis=1), block(f["w_branch_a_2"][0]),
           block(f["w_branch_b_2"][0])] + columns(f["w_out_2"][0]),
    ]
    wts = padded([b for m, q in zip(mixers, queries) for b in m + columns(q)])

    subs = [f["peer_sub_keys"][0], f["peer_sub_keys"][1],
            np.stack([f["peer_sub_keys_1_2"][0], f["peer_sub_keys_2_2"][0]], axis=1)]
    keys = np.stack([k.reshape(4, 4, N_KEYS, P).transpose(0, 3, 1, 2).reshape(4, P, 4 * N_KEYS) for k in subs])
    uvs = [np.concatenate([u, w], axis=1) for u, w in
           ((f["peer_u"][0], f["peer_v"][0]), (f["peer_u"][1], f["peer_v"][1]),
            (f["peer_expert_u_2"][0], f["peer_expert_v_2"][0]))]
    gains = np.stack([f["norm_mix"][0], f["norm_ffn"][0], f["norm_mix"][1], f["norm_ffn"][1],
                      f["mix_norm_g_2"][0], f["ffn_norm_g_2"][0], f["final_norm_g_2"]])
    small = np.concatenate([f["attn_q_norm"][0], f["attn_k_norm"][0], f["q_norm_g_2"][0], f["kv_norm_g_2"][0]])[None]

    f32 = np.float32
    p0 = np.arange(TILES * P, dtype=f32)[:, None]
    a0 = p0 * (f32(500000.0) ** (-np.arange(0, 16, 2, dtype=f32) / f32(16)))[None]
    rope0 = np.concatenate([np.cos(a0), np.sin(a0)], axis=1).astype(f32).reshape(TILES, P, 16).transpose(1, 0, 2)
    invf = np.concatenate([f32(10000.0) ** (-np.arange(0, n, 2, dtype=f32) / f32(n)) for n in (64, 32)])[None].astype(f32)
    q, k = np.arange(P)[:, None], np.arange(P)[None]
    causal = np.where(k <= q, 0.0, NEG)
    masks = np.stack([np.where(k > q, 0.0, NEG), causal, np.zeros((P, P)), causal], axis=1).astype(f32)

    arrays = {
        "x": f["x"].reshape(TILES * P, D), "wts": wts, "keys": keys, "gains": gains, "small": small,
        "sinks": f["attn_sinks"][0][order][None], "convw": f["conv_w"][0].reshape(3, KT, P).transpose(2, 1, 0),
        "pos": f["positions_2"].reshape(TILES, P).T, "rope0": rope0, "invf": invf,
        "iota": np.arange(TOPK, dtype=f32)[None], "ident": np.eye(P, dtype=f32), "masks": masks,
    }
    for l in range(LAYERS):
        arrays[f"uv{l}"] = uvs[l]
    arrays = {k: np.ascontiguousarray(v) for k, v in arrays.items()}

    nc = bacc.Bacc("TRN2", target_bir_lowering=False, num_devices=1)
    t = {k: nc.dram_tensor("in_" + k, v.shape, mybir.dt.from_np(v.dtype), kind="ExternalInput").ap() for k, v in arrays.items()}
    out = nc.dram_tensor("out", (TILES * P, D), F32, kind="ExternalOutput").ap()
    build(nc, t["x"], t["wts"], t["keys"], t["gains"], t["small"], t["sinks"], t["convw"], t["pos"], t["rope0"],
          t["invf"], t["iota"], t["ident"], t["masks"], [t[f"uv{l}"] for l in range(LAYERS)], out)
    got = run_bass_kernel_spmd(nc, [{"in_" + k: v for k, v in arrays.items()}], core_ids=[0]).results[0]["out"]
    return got.reshape(1, TILES * P, D)
```

```python
from contextlib import ExitStack

import numpy as np

import concourse.bass as bass
from concourse import mybir

F32 = mybir.dt.float32
U32 = mybir.dt.uint32
I32 = mybir.dt.int32
ACT = mybir.ActivationFunctionType
ALU = mybir.AluOpType
AXX = mybir.AxisListType.X

P = 128
D = 1024
KT = D // P
TILES = 2
LAYERS = 3
STEPS = LAYERS * TILES
EPS = 1e-6
NEG = -1e30

N_KEYS = 128
TOPK = 16
PEER_HEADS = 8
SLOTS = PEER_HEADS * TOPK
GROUP = 2
GROUPS = SLOTS // GROUP
PAIR = 2 * TOPK // GROUP
SPREAD = GROUPS - 1
MOVE_AT = 0
TURN = 8
BY_VECTOR = (3, 5, 6, 7)
RING = 10
DIAGS = 6
ACOLS = 16

BLK = 512
WBLK = KT * BLK

PI = float(np.float32(np.pi))
TWO_PI = 2.0 * np.pi
C1 = 6.28125
C2 = float(np.floor((TWO_PI - C1) * 2.0 ** 22) / 2.0 ** 22)
C3 = float(np.float32(TWO_PI - C1 - C2))
ROUND = 1.5 * 2.0 ** 23


def layer(s):
    return s // TILES


def tile(s):
    return s % TILES


W_BLOCKS = [
    [("qkv0", WBLK), ("qkv1", WBLK), ("qkv2", WBLK), ("out0", WBLK), ("out1", WBLK)],
    [(n, WBLK) for n in ("c0", "u0", "c1", "u1", "b0", "b1", "out0", "out1")],
    [("q", WBLK), ("k", WBLK), ("v", WBLK), ("lat", KT * 416), ("ga0", WBLK), ("ga1", WBLK),
     ("gb0", WBLK), ("gb1", WBLK), ("ups", 2 * 768 + 1024), ("bra", WBLK), ("brb", WBLK),
     ("out0", WBLK), ("out1", WBLK)],
]
W_BLOCKS = [b + [(f"q{i}", WBLK) for i in range(4)] for b in W_BLOCKS]
W_BASE = [sum(len(b) for b in W_BLOCKS[:i]) for i in range(LAYERS)]

HEADS = {"win": 16, "moba": 8, "mla": 8}
SCALE = {"win": 0.125, "moba": 0.125, "mla": float(96 ** -0.5)}
PARTS = [["win"], [], ["moba", "mla"]]


def heads_per_chunk(s):
    return BLK // (P * (tile(s) + 1))


def chunks(s, part):
    return HEADS[part] // heads_per_chunk(s)


def chunk_heads(s, part, c):
    hg = heads_per_chunk(s)
    if part == "mla":
        return slice(c * hg, (c + 1) * hg, 1)
    first = c % 2 + 2 * hg * (c // 2)
    return slice(first, first + 2 * hg - 1, 2)


def acc_uses(s):
    if layer(s) == 0:
        mixer = [("qkv0", "act"), ("qkv1", "act"), ("qkv2", "act"), ("o_win0", "dve"), ("o_win1", "dve"),
                 ("out0", "dve"), ("out1", "dve")]
    elif layer(s) == 1:
        mixer = [("c0", "act"), ("u0", "dve"), ("c1", "act"), ("u1", "dve"), ("b0", "dve"), ("b1", "dve"),
                 ("out0", "dve"), ("out1", "dve")]
    else:
        mixer = [(n, "act") for n in ("q", "k", "v", "lat", "ga0", "ga1", "gb0", "gb1")]
        mixer += [("o_moba0", "dve")] + [(n, "act") for n in ("uq0", "uq1", "uk", "uv")] + [("o_mla0", "dve")]
        mixer += [(n, "dve") for n in ("bra0", "brb0", "bra1", "brb1", "out0", "out1")]
    return mixer + [(f"q{i}", "act") for i in range(4)]


def transposes(s):
    out = ["mix0", "mix1"]
    for part in PARTS[layer(s)]:
        out += {"win": ["win_q0", "win_q1", "win_k"], "moba": ["moba_q", "moba_k"],
                "mla": ["lat", "mla_q0", "mla_q1", "mla_k0", "mla_k1"]}[part]
        out += [f"{part}_p{c}" for c in range(chunks(s, part))]
        out += {"win": ["win_o0", "win_o1"], "moba": [], "mla": ["o0", "o1"]}[part]
    if layer(s) == 2:
        out += ["mrg0", "mrg1"]
    return out + ["ffn0", "ffn1"]


def score_uses(s):
    return [f"{part}_s{c}" for part in PARTS[layer(s)] for c in range(chunks(s, part))] + [f"key{b}" for b in range(4)]


def pieces(s):
    def attention(part):
        return [f"{part}_chunk{c}" for c in range(chunks(s, part) + 1)] + [f"{part}_end"]

    if layer(s) == 0:
        mixer = ["mix_stat", "mix_T", "qkv0", "qk_norm0", "qkv1", "qk_norm1", "qkv2", "qk_norm2", "qk_T"] + attention("win")
        mixer += ["win_oT", "out0", "out1"]
    elif layer(s) == 1:
        mixer = ["mix_stat", "mix_T", "c0", "u0", "c1", "u1", "b0", "b1", "out0", "out1"]
    else:
        mixer = ["mix_stat", "mix_T", "q", "k", "v", "lat", "moba_rope", "ga0", "moba_T", "ga1", "gb0", "gb1"]
        mixer += attention("moba") + ["lat_norm", "lat_T", "uq0", "uq1", "uk", "uv", "mla_rope", "mla_T"]
        mixer += attention("mla") + ["oT", "br0", "br1", "mrg_T", "out0", "out1"]
    return mixer + ["ffn_stat", "ffn_T", "query0"] + [
        x for b in range(4) for x in (f"query{b + 1}", f"topA{b}", f"topB{b}", f"topC{b}")] + ["angles"] * (s == 0)


COST = {"window": 10.9, "topA": 2.6, "topB": 3.6, "topC": 4.0,
        "chunk": 2.2, "rope": 5.4, "norm": 1.4, "turn": 2.2, "end": 8.5, "product": 9.7}


def cost(p):
    if p.startswith("top"):
        return COST[p[:4]]
    if "_chunk" in p:
        return COST["window" if p.startswith("win") else "chunk"]
    if p.startswith("qk_norm"):
        return COST["rope"] / 2
    if p in ("moba_rope", "mla_rope", "u0", "u1", "angles"):
        return COST["rope"]
    if p.endswith(("_stat", "lat_norm")):
        return COST["norm"]
    if p.endswith("_end"):
        return COST["end"]
    if p.endswith(("_T", "oT")):
        return COST["turn"]
    return COST["product"]


def opening():
    out = [(0, p) for p in pieces(0)]
    for p, before in (("mix_stat", "qkv1"), ("mix_T", "qk_norm2"), ("qkv0", "qk_T"), ("qkv1", "win_chunk1"),
                      ("qkv2", "win_oT"), ("qk_norm0", "out0"), ("qk_norm1", "out0"), ("qk_norm2", "out0")):
        out.insert(out.index((0, before)), (1, p))
    return [("D", s, p) for s, p in out]


def schedule():
    out = []
    first = opening()
    ready = first.index(("D", 0, "topC0")) + 1
    out += first[:ready]
    waiting = first[ready:]
    for s in range(STEPS):
        todo = waiting + [("D", s + 1, p) for p in (pieces(s + 1) if s + 1 < STEPS else [])
                          if ("D", s + 1, p) not in first]
        waiting = []
        total = sum(cost(p) for _, _, p in todo)
        spent = 0.0
        for g in range(GROUPS):
            out.append(("G", s, g))
            if g == MOVE_AT and s > 0:
                out.append(("X", s - 1, 0))
            while todo and (g >= MOVE_AT or s == 0) and spent + cost(todo[0][2]) / 2 < total * (g + 1) / SPREAD:
                spent += cost(todo[0][2])
                out.append(todo.pop(0))
        out += todo
    out.append(("X", STEPS - 1, 0))
    return out


SCHEDULE = schedule()


OPENED = [(0, "mix"), (1, "mix"), (0, "mix0"), (0, "mix1"), (1, "mix0"), (1, "mix1"), (0, "qkv0"), (0, "qkv1"),
          (0, "qkv2"), (1, "qkv0"), (1, "qkv1"), (0, "o_win0"), (0, "o_win1"), (1, "qkv2")]


def in_order(per_step):
    events = [(s, label) for s, labels in enumerate(per_step) for label in labels]
    return [e for e in OPENED if e in events] + [e for e in events if e not in OPENED]


class Signal:

    def __init__(self, sem, per_step):
        self.sem = sem
        self.value = {event: n + 1 for n, event in enumerate(in_order(per_step))}

    def count(self, s, label):
        return self.value[s, label]


def build(nc, xin, wts, keys, gains, small, sinks, convw, pos, rope0, invf, iota, ident, masks, uv, out):
    ctx = ExitStack()
    with ctx:
        def sb(name, shape, dt=F32):
            return ctx.enter_context(nc.sbuf_tensor(name, shape, dt))

        def ps(name):
            return ctx.enter_context(nc.psum_tensor(name, [P, BLK], F32))

        def sem(name):
            return ctx.enter_context(nc.semaphore(name))

        steps = range(STEPS)

        ring = sb("ring", [P, RING, 2 * D])
        wbuf = sb("wbuf", [P, 2, WBLK])
        kbuf = sb("kbuf", [P, 2, BLK])
        x = sb("x", [P, TILES, D])
        h = sb("h", [P, TILES, D])
        fT = sb("fT", [P, KT, P])
        gain = sb("gain", [P, D])
        smallr = sb("smallr", [P, 512])
        sink = sb("sink", [P, 16])
        cw = sb("cw", [P, KT, 3])
        posi = sb("posi", [P, TILES], I32)
        posf = sb("posf", [P, TILES])
        rc = sb("rc", [P, TILES, 16])
        inv = sb("inv", [P, 48])
        cosr = sb("cosr", [P, TILES, 48])
        sinr = sb("sinr", [P, TILES, 48])
        iota_s = sb("iota_s", [P, TOPK])
        id_s = sb("id_s", [P, P])
        mask_s = sb("mask_s", [P, 4, P])
        epsc = sb("epsc", [P, 1])

        a = sb("a", [P, ACOLS])
        ge = sb("ge", [P, ACOLS])
        wgt = sb("wgt", [P, ACOLS])
        diag = sb("diag", [P, DIAGS, P])
        idx = sb("idx", [P, TILES, SLOTS], U32)
        gate = sb("gate", [P, TILES, SLOTS])

        big = sb("big", [P, 2 * D])
        qk = sb("qk", [P, 1440])
        oM = sb("oM", [P, D])
        qT = sb("qT", [P, KT, P])
        caches = sb("caches", [P, 5136])
        tmp = sb("tmp", [P, 1280])
        sm = sb("sm", [P, 2, BLK])
        pT = sb("pT", [P, 2, BLK])
        st = sb("st", [P, 16])
        r20 = sb("r20", [P, 40])
        mx = sb("mx", [P, 16])
        nmx = sb("nmx", [P, 16])
        den = sb("den", [P, 16])
        rden = sb("rden", [P, 16])
        esink = sb("esink", [P, 16])
        tv = sb("tv", [P, 4, TOPK])
        ti = sb("ti", [P, 4, TOPK], U32)
        tf = sb("tf", [P, 4, TOPK])
        best = sb("best", [P, 2, TOPK])
        nbest = sb("nbest", [P, 2])
        bsum = sb("bsum", [P, 2])
        posu = sb("posu", [P, 2, 2 * TOPK], U32)

        lat = qk[:, 1024:1440]
        ang = oM[:, 0:96].rearrange("p (t n) -> p t n", t=TILES)
        angk = oM[:, 96:192].rearrange("p (t n) -> p t n", t=TILES)
        queryT = qT[:, :, :].rearrange("p (b a) n -> p b (a n)", b=2)
        swork = sm[:, 0, :]
        isel = sm[:, 0, 0:4 * TOPK].rearrange("p (a n) -> p a n", a=2)
        posn = sm[:, 0, 4 * TOPK:8 * TOPK].rearrange("p (a n) -> p a n", a=2)
        cand = sm[:, 1, :].rearrange("p (a n) -> p a n", a=2)
        hot = pT[:, :, :].rearrange("p b n -> p (b n)").rearrange("p (a b c) -> p a b c", a=2, c=TOPK)

        c0_kT = caches[:, 0:512].rearrange("p (a n) -> p a n", a=2)
        c0_v = caches[:, 512:1024].rearrange("p (t n) -> p t n", t=TILES)
        qkv_new = [big[:, 0:1280], ring[:, RING - 1, 0:1280]]
        kept = caches[:, 1040:1040 + WBLK]
        z = caches[:, 0:KT * (P + 2)].rearrange("p (c n) -> p c n", c=KT)
        c2_kaT = caches[:, 0:1024].rearrange("p (a n) -> p a n", a=4)
        c2_va = caches[:, 1024:2048].rearrange("p (t n) -> p t n", t=TILES)
        c2_kbT = caches[:, 2048:4096].rearrange("p (a n) -> p a n", a=8)
        c2_vb = caches[:, 4096:5120].rearrange("p (t n) -> p t n", t=TILES)
        kfull = tmp[:, 0:768].rearrange("p (h n) -> p h n", h=8)

        y = [ps("y0"), ps("y1")]
        acc = [ps("acc0"), ps("acc1")]
        tp = [ps("tp0"), ps("tp1")]
        sc = [ps("sc0"), ps("sc1")]

        norms = [["mix", "ffn"] for s in steps]
        finals = [["final"] if layer(s) == LAYERS - 1 else [] for s in steps]
        const_in = sem("const_in")
        ident_in = sem("ident_in")
        x_in = [sem("x_in0"), sem("x_in1")]
        w_in = [sem("w_in0"), sem("w_in1")]
        kept_in = sem("kept_in")
        k_in = [sem("k_in0"), sem("k_in1")]
        gain_in = sem("gain_in")
        row_in = [sem(f"row_in{i}") for i in range(RING)]
        stored = sem("stored")
        dve_step = sem("dve_step")
        act_step = sem("act_step")
        acc_done = Signal(sem("acc_done"), [[n for n, _ in acc_uses(s)] for s in steps])
        acc_out = {e: Signal(sem(f"acc_out_{e}"), [[n for n, f in acc_uses(s) if f == e] for s in steps])
                   for e in ("act", "dve")}
        tp_done = Signal(sem("tp_done"), [transposes(s) for s in steps])
        tp_copied = Signal(sem("tp_copied"), [transposes(s) for s in steps])
        sc_done = Signal(sem("sc_done"), [score_uses(s) for s in steps])
        sc_read = Signal(sem("sc_read"), [score_uses(s) for s in steps])
        x_moved = Signal(sem("x_moved"), [["y"]] * STEPS)
        sq_ready = Signal(sem("sq_ready"), norms)
        h_ready = Signal(sem("h_ready"), norms)
        last_sq = Signal(sem("last_sq"), finals)
        out_ready = Signal(sem("out_ready"), finals)
        vector_part = Signal(sem("vector_part"), [
            {0: ["qk_sq0", "qk_norm0", "qk_sq1", "qk_norm1", "qk_sq2", "qk_norm2", "win_den"], 1: [],
             2: ["lat_sq", "moba_rope", "lat_norm", "mla_rope", "mrg"]}[layer(s)] for s in steps])
        scalar_part = Signal(sem("scalar_part"), [
            {0: ["qk_rms0", "qk_rms1", "qk_rms2", "win_esink"], 1: [], 2: ["lat_rms"]}[layer(s)] for s in steps])
        probs = Signal(sem("probs"), [[f"{p}_s{c}" for p in PARTS[layer(s)] for c in range(chunks(s, p))] for s in steps])
        max_done = Signal(sem("max_done"), [[f"{p}_s{c}" for p in PARTS[layer(s)] for c in range(chunks(s, p))] for s in steps])
        best_done = Signal(sem("best_done"), [range(4)] * STEPS)
        gate_exp = Signal(sem("gate_exp"), [range(4)] * STEPS)
        idx_ready = Signal(sem("idx_ready"), [range(4)] * STEPS)
        dots = Signal(sem("dots"), [range(GROUPS)] * STEPS)
        by_tensor = [k for k in range(SLOTS) if k % TURN not in BY_VECTOR]
        by_vector = [k for k in range(SLOTS) if k % TURN in BY_VECTOR]
        diags = Signal(sem("diags"), [by_tensor] * STEPS)
        y_slot = Signal(sem("y_slot"), [by_tensor] * STEPS)
        x_slot = Signal(sem("x_slot"), [by_vector] * STEPS)
        weights_at = Signal(sem("weights_at"), [range(GROUPS)] * STEPS)
        eps_ready = sem("eps_ready")
        trig_arg = sem("trig_arg")
        trig = sem("trig")

        N_CONST = 8
        opened = ("qkv1", "qkv2")
        y_uses = {(1, "qkv0"): 0, (1, "qkv1"): 1, (1, "qkv2"): 0}
        kept_blocks = [(0, "qkv0"), (0, "out0"), (1, "c0")]
        w_order = [(s, i) for s in steps for i, (name, _) in enumerate(W_BLOCKS[layer(s)])
                   if (layer(s), name) not in kept_blocks and not (s == 1 and name in opened)]
        w_index = {(s, W_BLOCKS[layer(s)][i][0]): n for n, (s, i) in enumerate(w_order)}
        w_index.update({(1, name): w_index[0, name] for name in opened})
        acc_order = [(s, n, e) for s in steps for n, e in acc_uses(s) if (s, n) not in y_uses]
        acc_index = {(s, n): i for i, (s, n, _) in enumerate(acc_order)}
        norm_order = [(s, n, 2 * layer(s) + (n == "ffn")) for s, n in in_order(norms)]
        gain_loads, gain_of = [], {}
        for i, (s, n, row) in enumerate(norm_order):
            if i == 0 or row != norm_order[i - 1][2]:
                gain_loads.append(i)
            gain_of[s, n] = len(gain_loads)
        tp_order = in_order([transposes(s) for s in steps])
        tp_index = {k: i for i, k in enumerate(tp_order)}
        sc_order = [(s, n) for s in steps for n in score_uses(s)]
        sc_index = {k: i for i, k in enumerate(sc_order)}
        at_order = [(s, f"{p}_s{c}") for s in steps for p in PARTS[layer(s)] for c in range(chunks(s, p))]
        at_index = {k: i for i, k in enumerate(at_order)}

        def acc_bank(s, name):
            return y[y_uses[s, name]] if (s, name) in y_uses else acc[acc_index[s, name] % 2]

        def tp_bank(s, name):
            return tp[tp_index[s, name] % 2]

        def sc_bank(s, name):
            return sc[sc_index[s, name] % 2]

        def keys_len(s):
            return P * (tile(s) + 1)

        def slot_done(engine, n):
            s, k = divmod(n, SLOTS)
            sig = x_slot if k % TURN in BY_VECTOR else y_slot
            engine.wait_ge(sig.sem, sig.count(s, k))

        block = ctx.enter_context(nc.Block())

        @block.sync
        def _(sp):
            def load_gain(s, which):
                i = norm_order.index((s, which, row := 2 * layer(s) + (which == "ffn")))
                if i not in gain_loads:
                    return
                if i:
                    sp.wait_ge(h_ready.sem, i)
                sp.dma_start(gain[:], gains[row:row + 1, :].broadcast_to([P, D])).then_inc(gain_in, 16)

            def load_x(t):
                sp.dma_start(x[:, t, :], xin[t * P:(t + 1) * P, :]).then_inc(x_in[t], 16)

            last_use = {"ups": "uv", "bra": "bra1", "brb": "brb1"}
            load_x(0)
            for s in steps:
                load_gain(s, "mix")
                if s == 0:
                    sp.dma_start(id_s[:], ident).then_inc(ident_in, 16)
                for i, (name, size) in enumerate(W_BLOCKS[layer(s)]):
                    if (layer(s), name) in kept_blocks and tile(s) == 0:
                        j = kept_blocks.index((layer(s), name))
                        if j:
                            l2, name2 = kept_blocks[j - 1]
                            sp.wait_ge(acc_done.sem, acc_done.count(TILES * l2 + 1, name2))
                        sp.dma_start(kept[:], wts[W_BASE[layer(s)] + i]).then_inc(kept_in, 16)
                    if (s, i) not in w_order:
                        continue
                    n = w_index[s, name]
                    if n >= 2:
                        s2, i2 = w_order[n - 2]
                        name2 = W_BLOCKS[layer(s2)][i2][0]
                        if s2 == 0 and name2 in opened:
                            s2 = 1
                        sp.wait_ge(acc_done.sem, acc_done.count(s2, last_use.get(name2, name2)))
                    sp.dma_start(wbuf[:, n % 2, 0:size], wts[W_BASE[layer(s)] + i, :, 0:size]).then_inc(w_in[n % 2], 16)
                    if n == 1:
                        load_x(1)
                        for dst, src in ((smallr[:], small.broadcast_to([P, 512])), (sink[:], sinks.broadcast_to([P, 16])),
                                         (cw[:], convw), (posi[:], pos), (rc[:], rope0),
                                         (inv[:], invf.broadcast_to([P, 48])), (iota_s[:], iota.broadcast_to([P, TOPK])),
                                         (mask_s[:], masks)):
                            sp.dma_start(dst, src).then_inc(const_in, 16)
                    if name == "out1":
                        load_gain(s, "ffn")
                    if name in ("q0", "q1", "q2", "q3"):
                        b = int(name[1])
                        m = 4 * s + b
                        if m >= 2:
                            sp.wait_ge(sc_done.sem, sc_done.count((m - 2) // 4, f"key{(m - 2) % 4}"))
                        sp.dma_start(kbuf[:, m % 2, :], keys[layer(s), b]).then_inc(k_in[m % 2], 16)
            sp.wait_ge(h_ready.sem, len(norm_order))
            sp.dma_start(gain[:], gains[2 * LAYERS:2 * LAYERS + 1, :].broadcast_to([P, D])).then_inc(gain_in, 16)
            for t in range(TILES):
                s = (LAYERS - 1) * TILES + t
                sp.wait_ge(out_ready.sem, out_ready.count(s, "final"))
                sp.dma_start(out[t * P:(t + 1) * P, :], h[:, t, :]).then_inc(stored, 16)
            sp.wait_ge(stored, 16 * TILES)

        @block.gpsimd
        def _(pool):
            for kind, s, g in SCHEDULE:
                if kind != "G":
                    continue
                if g % PAIR == 0:
                    pool.wait_ge(idx_ready.sem, idx_ready.count(s, g // PAIR))
                for k in range(g * GROUP, (g + 1) * GROUP):
                    n = s * SLOTS + k
                    if n >= RING:
                        slot_done(pool, n - RING)
                    nc.gpsimd.indirect_dma_start(
                        ring[:, n % RING, :], None, uv[layer(s)],
                        bass.IndirectOffsetOnAxis(ap=idx[:, tile(s), k:k + 1], axis=0),
                    ).then_inc(row_in[n % RING], 16)

        @block.tensor
        def _(pe):
            def acc_free(s, name):
                if (s, name) in y_uses:
                    if name == "qkv2":
                        pe.wait_ge(acc_out["act"].sem, acc_out["act"].count(s, "qkv0"))
                    return
                n = acc_index[s, name]
                if n >= 2:
                    s2, name2, e = acc_order[n - 2]
                    pe.wait_ge(acc_out[e].sem, acc_out[e].count(s2, name2))

            def tp_free(s, name):
                n = tp_index[s, name]
                if n >= 2:
                    pe.wait_ge(tp_copied.sem, n - 1)

            def sc_free(s, name):
                n = sc_index[s, name]
                if n >= 2:
                    pe.wait_ge(sc_read.sem, n - 1)

            def weights(s, name):
                if (layer(s), name) in kept_blocks:
                    pe.wait_ge(kept_in, 16 * (kept_blocks.index((layer(s), name)) + 1))
                    return kept[:]
                n = w_index[s, name]
                pe.wait_ge(w_in[n % 2], 16 * (n // 2 + 1))
                return wbuf[:, n % 2, :]

            def product(s, name, wname, cols=BLK, kts=range(KT), width=BLK, off=0, base=0):
                acc_free(s, name)
                w = weights(s, wname)
                for i, k in enumerate(kts):
                    mm = nc.tensor.matmul(acc_bank(s, name)[:, 0:cols], fT[:, k, :],
                                          w[:, base + i * width + off:base + i * width + off + cols],
                                          start=(i == 0), stop=(i == len(kts) - 1))
                mm.then_inc(acc_done.sem, 1)

            def product_T(s, name, wname):
                acc_free(s, name)
                w = weights(s, wname).rearrange("p (k n) -> p k n", k=KT)
                for j in range(4):
                    for k in range(KT):
                        mm = nc.tensor.matmul(acc_bank(s, name)[:, j * P:(j + 1) * P], w[:, k, j * P:(j + 1) * P],
                                              fT[:, k, :], start=(k == 0), stop=(k == KT - 1))
                mm.then_inc(acc_done.sem, 1)

            def turn(s, name, sources, rows=P):
                tp_free(s, name)
                for j, src in enumerate(sources):
                    mm = nc.tensor.transpose(tp_bank(s, name)[0:rows, j * P:(j + 1) * P], src, id_s[:])
                mm.then_inc(tp_done.sem, 1)

            def turn_rows(s, names, src):
                for i, name in enumerate(names):
                    turn(s, name, [src[:, (4 * i + j) * P:(4 * i + j + 1) * P] for j in range(4)])

            def scores(s, part, c):
                name = f"{part}_s{c}"
                sc_free(s, name)
                hg, kl = heads_per_chunk(s), keys_len(s)
                bank = sc_bank(s, name)
                hs = chunk_heads(s, part, c)
                for i, hd in enumerate(range(hs.start, hs.stop, hs.step)):
                    if part == "win":
                        b = hd % 2
                        lhs, rhs = qT[64 * b:64 * b + 64, hd // 2, :], c0_kT[64 * b:64 * b + 64, hd // 8, 0:kl]
                    elif part == "moba":
                        b = hd % 2
                        lhs, rhs = qT[64 * b:64 * b + 64, hd // 2, :], c2_kaT[64 * b:64 * b + 64, hd // 2, 0:kl]
                    else:
                        lhs, rhs = qT[0:96, hd, :], c2_kbT[0:96, hd, 0:kl]
                    mm = nc.tensor.matmul(bank[:, i * kl:(i + 1) * kl], lhs, rhs, start=True, stop=True)
                mm.then_inc(sc_done.sem, 1)

            def weigh(s, part, c):
                name = f"{part}_s{c}"
                hg, nk = heads_per_chunk(s), tile(s) + 1
                m = at_index[s, name]
                pe.wait_ge(probs.sem, probs.count(s, name))
                turn(s, f"{part}_p{c}", [sm[:, m % 2, j * P:(j + 1) * P] for j in range(4)])
                per_bank = 8
                hs = chunk_heads(s, part, c)
                o = f"o_{part}{hs.start // per_bank}"
                if c % (per_bank // hg) == 0:
                    acc_free(s, o)
                pe.wait_ge(tp_copied.sem, tp_copied.count(s, f"{part}_p{c}"))
                for i, hd in enumerate(range(hs.start, hs.stop, hs.step)):
                    for kt in range(nk):
                        if part == "win":
                            g = 2 * (hd // 8) + hd % 2
                            v = c0_v[:, kt, 64 * g:64 * g + 64]
                        else:
                            v = (c2_va if part == "moba" else c2_vb)[:, kt, 64 * hd:64 * hd + 64]
                        mm = nc.tensor.matmul(acc_bank(s, o)[:, (hd % per_bank) * 64:(hd % per_bank) * 64 + 64],
                                              pT[:, m % 2, (i * nk + kt) * P:(i * nk + kt + 1) * P], v,
                                              start=(kt == 0), stop=(kt == nk - 1))
                if (c + 1) % (per_bank // hg) == 0:
                    mm.then_inc(acc_done.sem, 1)

            def sub_keys(s, b):
                name = f"key{b}"
                m = 4 * s + b
                sc_free(s, name)
                pe.wait_ge(k_in[m % 2], 16 * (m // 2 + 1))
                pe.wait_ge(acc_out["act"].sem, acc_out["act"].count(s, f"q{b}"))
                for j in range(4):
                    mm = nc.tensor.matmul(sc_bank(s, name)[:, j * P:(j + 1) * P],
                                          queryT[:, m % 2, j * P:(j + 1) * P],
                                          kbuf[:, m % 2, j * P:(j + 1) * P], start=True, stop=True)
                mm.then_inc(sc_done.sem, 1)

            def dense(s, p):
                l = layer(s)
                if p == "mix_T":
                    if s == 0:
                        pe.wait_ge(ident_in, 16)
                    pe.wait_ge(h_ready.sem, h_ready.count(s, "mix"))
                    turn_rows(s, ["mix0", "mix1"], h[:, tile(s), :])
                elif p == "ffn_T":
                    pe.wait_ge(h_ready.sem, h_ready.count(s, "ffn"))
                    turn_rows(s, ["ffn0", "ffn1"], h[:, tile(s), :])
                elif p.startswith("query"):
                    b = int(p[5:])
                    if s == 0 and b > 0:
                        sub_keys(s, b - 1)
                    if b < 4:
                        if b == 0:
                            pe.wait_ge(tp_copied.sem, tp_copied.count(s, "ffn1"))
                        product_T(s, f"q{b}", f"q{b}")
                    if s > 0 and b > 0:
                        sub_keys(s, b - 1)
                elif p in ("qkv0", "qkv1", "qkv2") or (l == 2 and p in ("q", "k", "v", "lat", "ga0", "ga1", "gb0", "gb1")):
                    if p in ("qkv0", "q"):
                        pe.wait_ge(tp_copied.sem, tp_copied.count(s, "mix1"))
                    if p == "lat":
                        product(s, p, p, cols=416, width=416)
                    else:
                        product(s, p, p)
                elif l == 1 and p in ("c0", "u0", "c1", "u1", "b0", "b1"):
                    if p == "c0":
                        pe.wait_ge(tp_copied.sem, tp_copied.count(s, "mix1"))
                    product_T(s, p, p)
                elif p == "qk_T":
                    pe.wait_ge(vector_part.sem, vector_part.count(s, "qk_norm2"))
                    for i in range(2):
                        turn(s, f"win_q{i}", [big[:, (4 * i + j) * P:(4 * i + j + 1) * P] for j in range(4)])
                    turn(s, "win_k", [big[:, 1024 + j * P:1024 + (j + 1) * P] for j in range(2)])
                elif p == "moba_T":
                    pe.wait_ge(vector_part.sem, vector_part.count(s, "moba_rope"))
                    turn(s, "moba_q", [qk[:, j * P:(j + 1) * P] for j in range(4)])
                    turn(s, "moba_k", [qk[:, 512 + j * P:512 + (j + 1) * P] for j in range(4)])
                elif p == "lat_T":
                    pe.wait_ge(vector_part.sem, vector_part.count(s, "lat_norm"))
                    turn(s, "lat", [lat[:, j * P:(j + 1) * P] for j in range(3)])
                elif p in ("uq0", "uq1", "uk", "uv"):
                    if p == "uq0":
                        pe.wait_ge(tp_copied.sem, tp_copied.count(s, "lat"))
                    if p == "uq0":
                        product(s, p, "ups", kts=range(2), width=768)
                    elif p == "uq1":
                        product(s, p, "ups", cols=256, kts=range(2), width=768, off=512)
                    else:
                        product(s, p, "ups", kts=[2], base=2 * 768, off=512 * (p == "uv"))
                elif p == "mla_T":
                    pe.wait_ge(vector_part.sem, vector_part.count(s, "mla_rope"))
                    for i in range(2):
                        turn(s, f"mla_q{i}", [qk[:, (4 * i + j) * 96:(4 * i + j + 1) * 96] for j in range(4)], rows=96)
                    for i in range(2):
                        turn(s, f"mla_k{i}", [kfull[:, 4 * i + j, :] for j in range(4)], rows=96)
                elif "_chunk" in p:
                    part, c = p.split("_chunk")
                    c = int(c)
                    if c == 0:
                        last = {"win": "win_k", "moba": "moba_k", "mla": "mla_k1"}[part]
                        pe.wait_ge(tp_copied.sem, tp_copied.count(s, last))
                    for ahead in (0, 1) if c == 0 else (c + 1,):
                        if ahead < chunks(s, part):
                            scores(s, part, ahead)
                    if c > 0:
                        weigh(s, part, c - 1)
                elif p == "win_oT":
                    pe.wait_ge(acc_out["dve"].sem, acc_out["dve"].count(s, "o_win1"))
                    turn_rows(s, ["win_o0", "win_o1"], oM)
                elif p == "oT":
                    pe.wait_ge(acc_out["dve"].sem, acc_out["dve"].count(s, "o_mla0"))
                    turn_rows(s, ["o0", "o1"], oM)
                elif p in ("br0", "br1"):
                    n = int(p[2])
                    if n == 0:
                        pe.wait_ge(tp_copied.sem, tp_copied.count(s, "o1"))
                        weights(s, "bra")
                        weights(s, "brb")
                    for e, kts in (("bra", range(4)), ("brb", range(4, 8))):
                        product(s, f"{e}{n}", e, kts=kts, width=D, off=BLK * n)
                elif p == "mrg_T":
                    pe.wait_ge(vector_part.sem, vector_part.count(s, "mrg"))
                    turn_rows(s, ["mrg0", "mrg1"], oM)
                elif p in ("out0", "out1"):
                    if p == "out0":
                        if l == 1:
                            pe.wait_ge(acc_out["dve"].sem, acc_out["dve"].count(s, "b1"))
                        else:
                            pe.wait_ge(tp_copied.sem, tp_copied.count(s, "win_o1" if l == 0 else "mrg1"))
                    product(s, p, p)

            for kind, s, p in SCHEDULE:
                if kind == "D":
                    dense(s, p)
                elif kind == "G":
                    if p == 0 and s == 0:
                        pe.wait_ge(acc_out["act"].sem, acc_out["act"].count(1, "qkv2"))
                    if p == 0 and s > 0:
                        pe.wait_ge(x_moved.sem, x_moved.count(s - 1, "y"))
                    for k in range(p * GROUP, (p + 1) * GROUP):
                        if k % TURN in BY_VECTOR:
                            continue
                        n = s * SLOTS + k
                        d = diags.count(s, k)
                        pe.wait_ge(diags.sem, d)
                        for half in range(2):
                            mm = nc.tensor.matmul(y[half][:], diag[:, (d - 1) % DIAGS, :],
                                                  ring[:, n % RING, D + half * BLK:D + (half + 1) * BLK],
                                                  start=(k == by_tensor[0]), stop=(k == by_tensor[-1]))
                        mm.then_inc(y_slot.sem, 1)

        @block.scalar
        def _(act):
            n_act = [0]

            def mark(ins):
                n_act[0] += 1
                return ins.then_inc(act_step, 1)

            def settle():
                act.wait_ge(act_step, n_act[0])

            def copy(dst, src):
                return nc.scalar.activation(dst, src, ACT.Copy)

            def from_acc(s, name, dst, cols=BLK, func=ACT.Copy):
                act.wait_ge(acc_done.sem, acc_done.count(s, name))
                nc.scalar.activation(dst, acc_bank(s, name)[:, 0:cols], func).then_inc(acc_out["act"].sem, 1)

            def from_tp(s, name, dst, rows=P, cols=BLK):
                act.wait_ge(tp_done.sem, tp_done.count(s, name))
                src = tp_bank(s, name)[0:rows, 0:cols]
                if len(dst.shape) == 3:
                    src = src.rearrange("p (a n) -> p a n", a=dst.shape[1])
                copy(dst, src).then_inc(tp_copied.sem, 1)

            def root_mean_square(s, which):
                if which == "mix":
                    if s < TILES:
                        act.wait_ge(x_in[s], 16)
                    else:
                        act.wait_ge(x_moved.sem, x_moved.count(s - 2, "y"))
                elif which == "ffn":
                    act.wait_ge(acc_out["dve"].sem, acc_out["dve"].count(s, "out1"))
                else:
                    act.wait_ge(x_moved.sem, x_moved.count(s, "y"))
                mark(nc.scalar.activation(oM[:, 0:D], x[:, tile(s), :], ACT.Square, accum_out=st[:, 0:1]))
                settle()
                nc.scalar.activation(st[:, 1:2], st[:, 0:1], ACT.Sqrt, scale=1.0 / D,
                                     bias=epsc[:]).then_inc((last_sq if which == "final" else sq_ready).sem, 1)

            def dense(s, p):
                l, t = layer(s), tile(s)
                if p == "mix_stat":
                    root_mean_square(s, "mix")
                elif p == "angles":
                    act.wait_ge(trig_arg, 1)
                    nc.scalar.activation(sinr[:], ang[:], ACT.Sin).then_inc(trig, 1)
                    nc.scalar.activation(cosr[:], angk[:], ACT.Sin).then_inc(trig, 1)
                    act.wait_ge(trig, 2)
                elif p == "ffn_stat":
                    root_mean_square(s, "ffn")
                elif p == "mix_T":
                    for i in range(2):
                        from_tp(s, f"mix{i}", fT[:, 4 * i:4 * i + 4, :])
                elif p == "ffn_T":
                    for i in range(2):
                        from_tp(s, f"ffn{i}", fT[:, 4 * i:4 * i + 4, :])
                elif p.startswith("query") and p != "query4":
                    b = int(p[5:])
                    m = 4 * s + b
                    if m >= 2:
                        act.wait_ge(sc_done.sem, sc_done.count((m - 2) // 4, f"key{(m - 2) % 4}"))
                    from_acc(s, f"q{b}", queryT[:, m % 2, :])
                elif p.startswith("topB"):
                    b = int(p[4:])
                    act.wait_ge(best_done.sem, best_done.count(s, b))
                    for i in range(2):
                        e = nc.scalar.activation(gate[:, t, (2 * b + i) * TOPK:(2 * b + i + 1) * TOPK], best[:, i, :],
                                                 ACT.Exp, bias=nbest[:, i:i + 1], accum_out=bsum[:, i:i + 1])
                    e.then_inc(gate_exp.sem, 1)
                elif p in ("qkv0", "qkv1"):
                    from_acc(s, p, qkv_new[s % 2][:, 512 * int(p[3]):512 * int(p[3]) + 512])
                elif p == "qkv2":
                    act.wait_ge(acc_done.sem, acc_done.count(s, p))
                    mark(copy(qkv_new[s % 2][:, 1024:1280], acc_bank(s, p)[:, 0:256]))
                    copy(c0_v[:, t, :], acc_bank(s, p)[:, 256:512]).then_inc(acc_out["act"].sem, 1)
                elif p in ("qk_norm0", "qk_norm1", "qk_norm2"):
                    i = int(p[7])
                    act.wait_ge(vector_part.sem, vector_part.count(s, f"qk_sq{i}"))
                    h0, h1 = 8 * i, min(8 * i + 8, 20)
                    nc.scalar.activation(r20[:, 20 + h0:20 + h1], r20[:, h0:h1], ACT.Sqrt, scale=1.0 / 64,
                                         bias=epsc[:]).then_inc(scalar_part.sem, 1)
                elif p == "qk_T":
                    for i in range(2):
                        from_tp(s, f"win_q{i}", qT[:, 4 * i:4 * i + 4, :])
                    from_tp(s, "win_k", c0_kT[:, :, t * P:(t + 1) * P], cols=256)
                elif p == "moba_T":
                    from_tp(s, "moba_q", qT[:, 0:4, :])
                    from_tp(s, "moba_k", c2_kaT[:, :, t * P:(t + 1) * P])
                elif p == "mla_T":
                    for i in range(2):
                        from_tp(s, f"mla_q{i}", qT[0:96, 4 * i:4 * i + 4, :], rows=96)
                    for i in range(2):
                        from_tp(s, f"mla_k{i}", c2_kbT[0:96, 4 * i:4 * i + 4, t * P:(t + 1) * P], rows=96)
                elif "_chunk" in p:
                    part, c = p.split("_chunk")
                    c = int(c)
                    if c < chunks(s, part):
                        name = f"{part}_s{c}"
                        m = at_index[s, name] % 2
                        hg, kl = heads_per_chunk(s), keys_len(s)
                        act.wait_ge(max_done.sem, max_done.count(s, name))
                        hs = chunk_heads(s, part, c)
                        for i, hd in enumerate(range(hs.start, hs.stop, hs.step)):
                            e = nc.scalar.activation(sm[:, m, i * kl:(i + 1) * kl], sm[:, m, i * kl:(i + 1) * kl],
                                                     ACT.Exp, bias=nmx[:, hd:hd + 1], accum_out=den[:, hd:hd + 1])
                        e.then_inc(probs.sem, 1)
                    if c > 0:
                        name = f"{part}_s{c - 1}"
                        from_tp(s, f"{part}_p{c - 1}", pT[:, at_index[s, name] % 2, :])
                elif p == "win_end":
                    act.wait_ge(vector_part.sem, vector_part.count(s, "win_den"))
                    nc.scalar.activation(esink[:], esink[:], ACT.Exp).then_inc(scalar_part.sem, 1)
                elif p in ("win_oT", "oT", "mrg_T"):
                    n = {"win_oT": "win_o", "oT": "o", "mrg_T": "mrg"}[p]
                    for i in range(2):
                        from_tp(s, f"{n}{i}", fT[:, 4 * i:4 * i + 4, :])
                elif l == 1 and p in ("c0", "c1"):
                    act.wait_ge(acc_done.sem, acc_done.count(s, p))
                    copy(big[:, 512 * int(p[1]):512 * int(p[1]) + 512], acc_bank(s, p)[:]).then_inc(acc_out["act"].sem, 1)
                elif l == 2 and p in ("q", "k"):
                    from_acc(s, p, qk[:, 512 * (p == "k"):512 * (p == "k") + 512])
                elif l == 2 and p == "v":
                    from_acc(s, p, c2_va[:, t, :])
                elif p == "lat":
                    from_acc(s, p, lat[:], cols=416)
                elif p in ("ga0", "ga1", "gb0", "gb1"):
                    o = D * (p[1] == "b") + BLK * int(p[2])
                    from_acc(s, p, big[:, o:o + BLK], func=ACT.Sigmoid)
                elif p == "lat_norm":
                    act.wait_ge(vector_part.sem, vector_part.count(s, "lat_sq"))
                    mark(nc.scalar.activation(st[:, 6:7], st[:, 4:5], ACT.Sqrt, scale=1.0 / 256, bias=epsc[:]))
                    nc.scalar.activation(st[:, 7:8], st[:, 5:6], ACT.Sqrt, scale=1.0 / 128,
                                         bias=epsc[:]).then_inc(scalar_part.sem, 1)
                elif p == "lat_T":
                    from_tp(s, "lat", fT[:, 0:3, :], cols=3 * P)
                elif p in ("uq0", "uq1"):
                    from_acc(s, p, qk[:, 512 * int(p[2]):768 if p == "uq1" else 512], cols=256 if p == "uq1" else 512)
                elif p == "uk":
                    act.wait_ge(acc_done.sem, acc_done.count(s, p))
                    copy(kfull[:, :, 0:64], acc_bank(s, p)[:].rearrange("p (h n) -> p h n", h=8))\
                        .then_inc(acc_out["act"].sem, 1)
                elif p == "uv":
                    from_acc(s, p, c2_vb[:, t, :])

            act.wait_ge(eps_ready, 1)
            nc.scalar.activation(st[:, 3:4], epsc[:], ACT.Sqrt)
            act.wait_ge(ident_in, 16)
            for kind, s, p in SCHEDULE:
                if kind == "D":
                    dense(s, p)
                elif kind == "G":
                    if p % PAIR == 0:
                        act.wait_ge(idx_ready.sem, idx_ready.count(s, p // PAIR))
                    k0 = p * GROUP
                    n0 = s * SLOTS + k0
                    c0 = n0 % ACOLS
                    act.wait_ge(dots.sem, dots.count(s, p))
                    mark(nc.scalar.activation(ge[:, c0:c0 + GROUP], a[:, c0:c0 + GROUP], ACT.Gelu))
                    settle()
                    for i in range(GROUP):
                        last = nc.scalar.activation(wgt[:, c0 + i:c0 + i + 1], ge[:, c0 + i:c0 + i + 1], ACT.Copy,
                                                    scale=gate[:, tile(s), k0 + i:k0 + i + 1])
                    last.then_inc(weights_at.sem, 1)
                    act.wait_ge(weights_at.sem, weights_at.count(s, p))
                    for i in range(GROUP):
                        if (k0 + i) % TURN in BY_VECTOR:
                            continue
                        d = diags.count(s, k0 + i)
                        if d > DIAGS:
                            act.wait_ge(y_slot.sem, d - DIAGS)
                        nc.scalar.activation(diag[:, (d - 1) % DIAGS, :], id_s[:], ACT.Copy,
                                             scale=wgt[:, c0 + i:c0 + i + 1]).then_inc(diags.sem, 1)
                elif kind == "X" and layer(s) == LAYERS - 1:
                    root_mean_square(s, "final")

        @block.vector
        def _(dve):
            n_dve = [0]
            v = nc.vector

            def mark(ins):
                n_dve[0] += 1
                return ins.then_inc(dve_step, 1)

            def settle():
                dve.wait_ge(dve_step, n_dve[0])

            def link(ins):
                mark(ins)
                settle()

            def norm(s, which):
                rms = last_sq if which == "final" else sq_ready
                if which == "mix" and s < TILES:
                    dve.wait_ge(x_in[s], 16)
                dve.wait_ge(rms.sem, rms.count(s, which))
                link(v.reciprocal(st[:, 2:3], st[:, 1:2]))
                dve.wait_ge(gain_in, 16 * (len(gain_loads) + 1 if which == "final" else gain_of[s, which]))
                ins = v.scalar_tensor_tensor(h[:, tile(s), :], x[:, tile(s), :], st[:, 2:3], gain[:], ALU.mult, ALU.mult)
                return ins

            def rope(x1, x2, o1, o2, cos, sin, n, w, scratch):
                t1, t2, t3, t4 = [scratch[:, i * n * w:(i + 1) * n * w].rearrange("p (h n) -> p h n", h=n) for i in range(4)]
                cb, sb_ = cos.unsqueeze(1).broadcast_to([P, n, w]), sin.unsqueeze(1).broadcast_to([P, n, w])
                mark(v.tensor_tensor(t1, x1, cb, ALU.mult))
                mark(v.tensor_tensor(t2, x2, sb_, ALU.mult))
                mark(v.tensor_tensor(t3, x2, cb, ALU.mult))
                mark(v.tensor_tensor(t4, x1, sb_, ALU.mult))
                settle()
                mark(v.tensor_tensor(o1, t1, t2, ALU.subtract))
                return v.tensor_tensor(o2, t3, t4, ALU.add)

            def softmax_chunk(s, part, c):
                name = f"{part}_s{c}"
                hg, kl = heads_per_chunk(s), keys_len(s)
                m = at_index[s, name]
                dve.wait_ge(sc_done.sem, sc_done.count(s, name))
                if m >= 2:
                    s2, name2 = at_order[m - 2]
                    dve.wait_ge(tp_done.sem, tp_done.count(s2, name2.replace("_s", "_p")))
                if tile(s) == 0:
                    mk = mask_s[:, 1, :]
                else:
                    mk = (mask_s[:, 0:2, :] if part == "win" else mask_s[:, 2:4, :]).rearrange("p a n -> p (a n)")
                smv = sm[:, m % 2, :].rearrange("p (h n) -> p h n", h=hg)
                v.scalar_tensor_tensor(smv, sc_bank(s, name)[:].rearrange("p (h n) -> p h n", h=hg), SCALE[part],
                                       mk.unsqueeze(1).broadcast_to([P, hg, kl]), ALU.mult, ALU.add)\
                    .then_inc(sc_read.sem, 1)
                dve.wait_ge(sc_read.sem, sc_read.count(s, name))
                hs = chunk_heads(s, part, c)
                link(v.tensor_reduce(mx[:, hs], smv, AXX, ALU.max))
                if part == "win":
                    link(v.tensor_tensor(mx[:, hs], mx[:, hs], sink[:, hs], ALU.max))
                v.tensor_scalar(nmx[:, hs], mx[:, hs], -1.0, None, ALU.mult).then_inc(max_done.sem, 1)

            def out_of_attention(s, part, col):
                n = HEADS[part]
                link(v.reciprocal(rden[:, 0:n], den[:, 0:n]))
                for half in range(n // 8):
                    o = f"o_{part}{half}"
                    dve.wait_ge(acc_done.sem, acc_done.count(s, o))
                    v.tensor_tensor(oM[:, col + half * BLK:col + (half + 1) * BLK].rearrange("p (h n) -> p h n", h=8),
                                    acc_bank(s, o)[:].rearrange("p (h n) -> p h n", h=8),
                                    rden[:, half * 8:half * 8 + 8].unsqueeze(2).broadcast_to([P, 8, 64]), ALU.mult)\
                        .then_inc(acc_out["dve"].sem, 1)

            def halves_best(s, b):
                name = f"key{b}"
                dve.wait_ge(sc_done.sem, sc_done.count(s, name))
                keys_of = [sc_bank(s, name)[:, j * P:(j + 1) * P] for j in range(4)]
                rest_of = [swork[:, j * P:(j + 1) * P] for j in range(4)]
                for j in range(4):
                    mark(v.max(tv[:, j, 0:8], keys_of[j]))
                settle()
                for j in range(4):
                    mark(v.max_index(ti[:, j, 0:8], tv[:, j, 0:8], keys_of[j]))
                for j in range(4):
                    ins = v.match_replace(rest_of[j], tv[:, j, 0:8], keys_of[j], -3e38)
                ins.then_inc(sc_read.sem, 1)
                dve.wait_ge(sc_read.sem, sc_read.count(s, name))
                for j in range(4):
                    mark(v.max(tv[:, j, 8:16], rest_of[j]))
                settle()
                for j in range(4):
                    mark(v.max_index(ti[:, j, 8:16], tv[:, j, 8:16], rest_of[j]))

            def sums_best(s, b):
                settle()
                for i in range(2):
                    mark(v.tensor_tensor(cand[:, i, :].rearrange("p (a b) -> p a b", a=TOPK),
                                         tv[:, 2 * i, :].unsqueeze(2).broadcast_to([P, TOPK, TOPK]),
                                         tv[:, 2 * i + 1, :].unsqueeze(1).broadcast_to([P, TOPK, TOPK]), ALU.add))
                settle()
                mark(v.tensor_copy(tf[:], ti[:]))
                rest2 = [hot[:, i, 0:TOPK, :].rearrange("p a b -> p (a b)") for i in range(2)]
                for i in range(2):
                    mark(v.max(best[:, i, 0:8], cand[:, i, :]))
                settle()
                for i in range(2):
                    mark(v.max_index(posu[:, i, 0:8], best[:, i, 0:8], cand[:, i, :]))
                    mark(v.match_replace(rest2[i], best[:, i, 0:8], cand[:, i, :], -3e38))
                v.tensor_scalar(nbest[:], best[:, :, 0], -1.0, None, ALU.mult)
                settle()
                for i in range(2):
                    ins = v.max(best[:, i, 8:16], rest2[i])
                ins.then_inc(best_done.sem, 1)
                dve.wait_ge(best_done.sem, best_done.count(s, b))
                for i in range(2):
                    mark(v.max_index(posu[:, i, 8:16], best[:, i, 8:16], rest2[i]))

            def experts(s, b):
                t = tile(s)
                settle()
                link(v.tensor_scalar(posu[:, :, TOPK:], posu[:, :, 0:TOPK], 15, None, ALU.bitwise_and))
                link(v.tensor_scalar(posu[:, :, 0:TOPK], posu[:, :, 0:TOPK], 4, None, ALU.logical_shift_right))
                link(v.tensor_copy(posn[:], posu[:]))
                link(v.tensor_tensor(hot[:].rearrange("p a b c -> p (a b) c"),
                                     posn[:].rearrange("p a b -> p (a b)").unsqueeze(2).broadcast_to([P, 4 * TOPK, TOPK]),
                                     iota_s[:].unsqueeze(1).broadcast_to([P, 4 * TOPK, TOPK]), ALU.is_equal))
                hot4 = hot[:].rearrange("p a (u b) c -> p (a u) b c", u=2)
                link(v.tensor_tensor(hot4, hot4, tf[:].unsqueeze(2).broadcast_to([P, 4, TOPK, TOPK]), ALU.mult))
                link(v.tensor_reduce(isel[:].rearrange("p a b -> p (a b)"), hot[:].rearrange("p a b c -> p (a b) c"),
                                     AXX, ALU.add))
                cols = slice(2 * b * TOPK, (2 * b + 2) * TOPK)
                mark(v.scalar_tensor_tensor(idx[:, t, cols].rearrange("p (a b) -> p a b", a=2), isel[:, :, 0:TOPK],
                                            float(N_KEYS), isel[:, :, TOPK:], ALU.mult, ALU.add))
                dve.wait_ge(gate_exp.sem, gate_exp.count(s, b))
                link(v.reciprocal(bsum[:], bsum[:]))
                gv = gate[:, t, cols].rearrange("p (a b) -> p a b", a=2)
                v.tensor_tensor(gv, gv, bsum[:].unsqueeze(2).broadcast_to([P, 2, TOPK]), ALU.mult)\
                    .then_inc(idx_ready.sem, 1)

            def add_rows(s, g):
                mine = [k for k in range(g * GROUP, (g + 1) * GROUP) if k in by_vector]
                if mine:
                    dve.wait_ge(weights_at.sem, weights_at.count(s, g))
                for k in mine:
                    n = s * SLOTS + k
                    m = x_slot.count(s, k)
                    if m > 1:
                        dve.wait_ge(x_slot.sem, m - 1)
                    xs = x[:, tile(s), :]
                    v.scalar_tensor_tensor(xs, ring[:, n % RING, D:2 * D], wgt[:, n % ACOLS:n % ACOLS + 1], xs,
                                           ALU.mult, ALU.add).then_inc(x_slot.sem, 1)

            def add_to_x(s, half, name):
                dve.wait_ge(acc_done.sem, acc_done.count(s, name))
                xs = x[:, tile(s), half * BLK:(half + 1) * BLK]
                v.tensor_tensor(xs, xs, acc_bank(s, name)[:], ALU.add).then_inc(acc_out["dve"].sem, 1)

            def angles():
                link(v.tensor_copy(posf[:], posi[:]))
                for t in range(TILES):
                    mark(v.tensor_scalar(ang[:, t, :], inv[:], posf[:, t:t + 1], None, ALU.mult))
                settle()
                link(v.tensor_scalar(angk[:], ang[:], 1.0 / TWO_PI, ROUND, ALU.mult, ALU.add))
                link(v.tensor_scalar(angk[:], angk[:], -ROUND, None, ALU.add))
                for c in (C1, C2, C3):
                    link(v.scalar_tensor_tensor(ang[:], angk[:], -c, ang[:], ALU.mult, ALU.add))
                link(v.tensor_scalar(ang[:], ang[:], PI, -PI, ALU.min, ALU.max))
                link(v.scalar_tensor_tensor(angk[:], ang[:], -1.0, ang[:], ALU.mult, ALU.max))
                v.tensor_scalar(angk[:], angk[:], -1.0, PI / 2, ALU.mult, ALU.add).then_inc(trig_arg, 1)

            def dense(s, p):
                l, t = layer(s), tile(s)
                if p == "mix_stat":
                    norm(s, "mix").then_inc(h_ready.sem, 1)
                elif p == "angles":
                    angles()
                elif p == "ffn_stat":
                    norm(s, "ffn").then_inc(h_ready.sem, 1)
                elif p.startswith("top"):
                    {"A": halves_best, "B": sums_best, "C": experts}[p[3]](s, int(p[4:]))
                elif p in ("out0", "out1"):
                    add_to_x(s, int(p[3]), p)
                elif p in ("qk_norm0", "qk_norm1", "qk_norm2"):
                    i = int(p[7])
                    h0, n = 8 * i, 4 if i == 2 else 8
                    if s == 0 and i == 0:
                        dve.wait_ge(const_in, 16 * N_CONST)
                    dve.wait_ge(acc_out["act"].sem, acc_out["act"].count(s, f"qkv{i}"))
                    qkv = big[:, 64 * h0:64 * (h0 + n)].rearrange("p (h n) -> p h n", h=n)
                    new = qkv_new[t][:, 64 * h0:64 * (h0 + n)].rearrange("p (h n) -> p h n", h=n)
                    sq = qk[:, 0:64 * n].rearrange("p (h n) -> p h n", h=n)
                    if t == 1 and i == 0:
                        dve.wait_ge(tp_done.sem, tp_done.count(0, "win_k"))
                    if i > 0:
                        dve.wait_ge(vector_part.sem, vector_part.count(s, f"qk_norm{i - 1}"))
                    link(v.tensor_tensor(sq, new, new, ALU.mult))
                    v.tensor_reduce(r20[:, h0:h0 + n], sq, AXX, ALU.add).then_inc(vector_part.sem, 1)
                    dve.wait_ge(scalar_part.sem, scalar_part.count(s, f"qk_rms{i}"))
                    link(v.reciprocal(r20[:, h0:h0 + n], r20[:, 20 + h0:20 + h0 + n]))
                    link(v.tensor_tensor(qkv, new, r20[:, h0:h0 + n].unsqueeze(2).broadcast_to([P, n, 64]), ALU.mult))
                    g0 = 64 if i == 2 else 0
                    link(v.tensor_tensor(qkv, qkv, smallr[:, g0:g0 + 64].unsqueeze(1).broadcast_to([P, n, 64]), ALU.mult))
                    rope(qkv[:, :, 0:8], qkv[:, :, 8:16], qkv[:, :, 0:8], qkv[:, :, 8:16],
                         rc[:, t, 0:8], rc[:, t, 8:16], n, 8, qk).then_inc(vector_part.sem, 1)
                elif "_chunk" in p:
                    part, c = p.split("_chunk")
                    if int(c) < chunks(s, part):
                        softmax_chunk(s, part, int(c))
                elif p == "win_end":
                    dve.wait_ge(max_done.sem, max_done.count(s, f"win_s{chunks(s, 'win') - 1}"))
                    v.tensor_tensor(esink[:], nmx[:], sink[:], ALU.add).then_inc(vector_part.sem, 1)
                    dve.wait_ge(scalar_part.sem, scalar_part.count(s, "win_esink"))
                    link(v.tensor_tensor(den[:], den[:], esink[:], ALU.add))
                    out_of_attention(s, "win", 0)
                elif p == "moba_end":
                    dve.wait_ge(probs.sem, probs.count(s, f"moba_s{chunks(s, 'moba') - 1}"))
                    out_of_attention(s, "moba", 0)
                elif p == "mla_end":
                    dve.wait_ge(probs.sem, probs.count(s, f"mla_s{chunks(s, 'mla') - 1}"))
                    out_of_attention(s, "mla", 512)
                elif l == 1 and p in ("u0", "u1"):
                    j = int(p[1])
                    z4 = z[:, 4 * j:4 * j + 4, :]
                    if t == 0:
                        mark(v.memset(z4[:, :, 0:2], 0.0))
                    else:
                        mark(v.tensor_copy(z4[:, :, 0:2], z4[:, :, P:P + 2]))
                        settle()
                    dve.wait_ge(acc_out["act"].sem, acc_out["act"].count(s, f"c{j}"))
                    dve.wait_ge(acc_done.sem, acc_done.count(s, p))
                    v.tensor_tensor(z4[:, :, 2:P + 2], acc_bank(s, p)[:].rearrange("p (c n) -> p c n", c=4),
                                    big[:, 512 * j:512 * j + 512].rearrange("p (c n) -> p c n", c=4), ALU.mult)\
                        .then_inc(acc_out["dve"].sem, 1)
                    dve.wait_ge(acc_out["dve"].sem, acc_out["dve"].count(s, p))
                    settle()
                    cv = big[:, D + 512 * j:D + 512 * j + 512].rearrange("p (c n) -> p c n", c=4)
                    tv4 = tmp[:, 0:512].rearrange("p (c n) -> p c n", c=4)
                    for i in range(3):
                        link(v.tensor_tensor(tv4 if i else cv, z4[:, :, i:i + P],
                                             cw[:, 4 * j:4 * j + 4, i].unsqueeze(2).broadcast_to([P, 4, P]), ALU.mult))
                        if i:
                            link(v.tensor_tensor(cv, cv, tv4, ALU.add))
                elif l == 1 and p == "b1":
                    dve.wait_ge(acc_done.sem, acc_done.count(s, "b1"))
                    for j in range(2):
                        v.tensor_tensor(fT[:, 4 * j:4 * j + 4, :].rearrange("p c n -> p (c n)"), acc_bank(s, f"b{j}")[:],
                                        big[:, D + 512 * j:D + 512 * j + 512], ALU.mult).then_inc(acc_out["dve"].sem, 1)
                elif p == "moba_rope":
                    dve.wait_ge(acc_out["act"].sem, acc_out["act"].count(s, "k"))
                    dve.wait_ge(trig, 2)
                    dve.wait_ge(vector_part.sem, vector_part.count(s, "lat_sq"))
                    q3 = qk[:, 0:1024].rearrange("p (h n) -> p h n", h=16)
                    for i in range(2):
                        hs = slice(8 * i, 8 * i + 8)
                        last = rope(q3[:, hs, 0:32], q3[:, hs, 32:64], q3[:, hs, 0:32], q3[:, hs, 32:64],
                                    cosr[:, t, 0:32], sinr[:, t, 0:32], 8, 32, tmp)
                        if i == 0:
                            link(last)
                    last.then_inc(vector_part.sem, 1)
                elif p == "lat":
                    dve.wait_ge(acc_out["act"].sem, acc_out["act"].count(s, "lat"))
                    mark(v.tensor_tensor_reduce(tmp[:, 0:256], lat[:, 0:256], lat[:, 0:256], 1.0, 0.0, ALU.mult, ALU.add,
                                                st[:, 4:5]))
                    v.tensor_tensor_reduce(tmp[:, 256:384], lat[:, 256:384], lat[:, 256:384], 1.0, 0.0, ALU.mult,
                                           ALU.add, st[:, 5:6]).then_inc(vector_part.sem, 1)
                elif p == "lat_norm":
                    dve.wait_ge(scalar_part.sem, scalar_part.count(s, "lat_rms"))
                    link(v.reciprocal(st[:, 8:10], st[:, 6:8]))
                    mark(v.scalar_tensor_tensor(lat[:, 0:256], lat[:, 0:256], st[:, 8:9], smallr[:, 128:384],
                                                ALU.mult, ALU.mult))
                    v.scalar_tensor_tensor(lat[:, 256:384], lat[:, 256:384], st[:, 9:10], smallr[:, 384:512],
                                           ALU.mult, ALU.mult).then_inc(vector_part.sem, 1)
                elif p == "mla_rope":
                    cb, sb_ = cosr[:, t, 32:48], sinr[:, t, 32:48]
                    l3 = lat[:, 384:416].unsqueeze(1)
                    scratch = tmp[:, 768:1280]
                    dve.wait_ge(acc_out["act"].sem, acc_out["act"].count(s, "uk"))
                    link(rope(l3[:, :, 0:16], l3[:, :, 16:32], l3[:, :, 0:16], l3[:, :, 16:32], cb, sb_, 1, 16, scratch))
                    mark(v.tensor_copy(kfull[:, :, 64:96], lat[:, 384:416].unsqueeze(1).broadcast_to([P, 8, 32])))
                    q3 = qk[:, 0:768].rearrange("p (h n) -> p h n", h=8)
                    rope(q3[:, :, 64:80], q3[:, :, 80:96], q3[:, :, 64:80], q3[:, :, 80:96], cb, sb_, 8, 16, scratch)\
                        .then_inc(vector_part.sem, 1)
                elif p in ("br0", "br1"):
                    n = int(p[2])
                    dst = oM[:, n * BLK:(n + 1) * BLK]
                    dve.wait_ge(acc_done.sem, acc_done.count(s, f"bra{n}"))
                    v.tensor_tensor(dst, acc_bank(s, f"bra{n}")[:], big[:, n * BLK:(n + 1) * BLK], ALU.mult)\
                        .then_inc(acc_out["dve"].sem, 1)
                    dve.wait_ge(acc_done.sem, acc_done.count(s, f"brb{n}"))
                    v.tensor_tensor(tmp[:, 0:BLK], acc_bank(s, f"brb{n}")[:], big[:, D + n * BLK:D + (n + 1) * BLK],
                                    ALU.mult).then_inc(acc_out["dve"].sem, 1)
                    dve.wait_ge(acc_out["dve"].sem, acc_out["dve"].count(s, f"brb{n}"))
                    last = v.tensor_tensor(dst, dst, tmp[:, 0:BLK], ALU.add)
                    if n == 0:
                        link(last)
                    else:
                        last.then_inc(vector_part.sem, 1)

            v.memset(epsc[:], EPS).then_inc(eps_ready, 1)
            for kind, s, p in SCHEDULE:
                if kind == "D":
                    dense(s, p)
                elif kind == "G":
                    for k in range(p * GROUP, (p + 1) * GROUP):
                        n = s * SLOTS + k
                        c = n % ACOLS
                        dve.wait_ge(row_in[n % RING], 16 * (n // RING + 1))
                        u = ring[:, n % RING, 0:D]
                        ins = v.tensor_tensor_reduce(u, u, h[:, tile(s), :], 1.0, 0.0, ALU.mult, ALU.add, a[:, c:c + 1])
                    ins.then_inc(dots.sem, 1)
                    if p > 0:
                        add_rows(s, p - 1)
                else:
                    add_rows(s, GROUPS - 1)
                    dve.wait_ge(x_slot.sem, x_slot.count(s, by_vector[-1]))
                    dve.wait_ge(y_slot.sem, y_slot.count(s, by_tensor[-1]))
                    for half in range(2):
                        xs = x[:, tile(s), half * BLK:(half + 1) * BLK]
                        last = v.tensor_tensor(xs, xs, y[half][:], ALU.add)
                    last.then_inc(x_moved.sem, 1)
                    if layer(s) == LAYERS - 1:
                        norm(s, "final").then_inc(out_ready.sem, 1)


def kernel(**inputs):
    import concourse.bacc as bacc
    from concourse.bass_utils import run_bass_kernel_spmd

    f = {k: np.asarray(v) for k, v in inputs.items()}

    def block(w):
        k, n = w.shape
        flat = w.reshape(k // P, P, n).transpose(1, 0, 2).reshape(P, -1)
        return flat

    def padded(blocks):
        out = np.zeros((len(blocks), P, WBLK), np.float32)
        for i, b in enumerate(blocks):
            out[i, :, :b.shape[1]] = b
        return out

    def columns(w):
        return [block(w[:, i:i + BLK]) for i in range(0, w.shape[1], BLK)]

    order = np.arange(16).reshape(2, 2, 4).transpose(0, 2, 1).reshape(-1)
    w_qkv, w_o = f["attn_w_qkv"][0], f["attn_w_o"][0]
    w_q = w_qkv[:, :D].reshape(D, 16, 64)[:, order].reshape(D, D)
    w_o = w_o.reshape(16, 64, D)[order].reshape(D, D)
    win = f["w_in_2"][0]
    kv_up = f["w_kv_up_2"][0].reshape(P, 8, 2, 64).transpose(0, 2, 1, 3).reshape(P, D)
    cin = f["conv_w_in"][0]
    queries = [f["peer_w_query"][0], f["peer_w_query"][1], f["w_peer_query_2"][0]]
    mixers = [
        columns(w_q) + columns(w_qkv[:, D:]) + columns(w_o),
        columns(np.concatenate([cin[:, D:D + BLK], cin[:, 2 * D:2 * D + BLK], cin[:, D + BLK:2 * D],
                                cin[:, 2 * D + BLK:], cin[:, :D]], axis=1)) + columns(f["conv_w_out"][0]),
        columns(win[:, :1536]) + [block(win[:, 1536:1952])] + columns(win[:, 1952:])
        + [np.concatenate([block(f["w_q_up_2"][0]), kv_up], axis=1), block(f["w_branch_a_2"][0]),
           block(f["w_branch_b_2"][0])] + columns(f["w_out_2"][0]),
    ]
    wts = padded([b for m, q in zip(mixers, queries) for b in m + columns(q)])

    subs = [f["peer_sub_keys"][0], f["peer_sub_keys"][1],
            np.stack([f["peer_sub_keys_1_2"][0], f["peer_sub_keys_2_2"][0]], axis=1)]
    keys = np.stack([k.reshape(4, 4, N_KEYS, P).transpose(0, 3, 1, 2).reshape(4, P, 4 * N_KEYS) for k in subs])
    uvs = [np.concatenate([u, w], axis=1) for u, w in
           ((f["peer_u"][0], f["peer_v"][0]), (f["peer_u"][1], f["peer_v"][1]),
            (f["peer_expert_u_2"][0], f["peer_expert_v_2"][0]))]
    gains = np.stack([f["norm_mix"][0], f["norm_ffn"][0], f["norm_mix"][1], f["norm_ffn"][1],
                      f["mix_norm_g_2"][0], f["ffn_norm_g_2"][0], f["final_norm_g_2"]])
    small = np.concatenate([f["attn_q_norm"][0], f["attn_k_norm"][0], f["q_norm_g_2"][0], f["kv_norm_g_2"][0]])[None]

    f32 = np.float32
    p0 = np.arange(TILES * P, dtype=f32)[:, None]
    a0 = p0 * (f32(500000.0) ** (-np.arange(0, 16, 2, dtype=f32) / f32(16)))[None]
    rope0 = np.concatenate([np.cos(a0), np.sin(a0)], axis=1).astype(f32).reshape(TILES, P, 16).transpose(1, 0, 2)
    invf = np.concatenate([f32(10000.0) ** (-np.arange(0, n, 2, dtype=f32) / f32(n)) for n in (64, 32)])[None].astype(f32)
    q, k = np.arange(P)[:, None], np.arange(P)[None]
    causal = np.where(k <= q, 0.0, NEG)
    masks = np.stack([np.where(k > q, 0.0, NEG), causal, np.zeros((P, P)), causal], axis=1).astype(f32)

    arrays = {
        "x": f["x"].reshape(TILES * P, D), "wts": wts, "keys": keys, "gains": gains, "small": small,
        "sinks": f["attn_sinks"][0][order][None], "convw": f["conv_w"][0].reshape(3, KT, P).transpose(2, 1, 0),
        "pos": f["positions_2"].reshape(TILES, P).T, "rope0": rope0, "invf": invf,
        "iota": np.arange(TOPK, dtype=f32)[None], "ident": np.eye(P, dtype=f32), "masks": masks,
    }
    for l in range(LAYERS):
        arrays[f"uv{l}"] = uvs[l]
    arrays = {k: np.ascontiguousarray(v) for k, v in arrays.items()}

    nc = bacc.Bacc("TRN2", target_bir_lowering=False, num_devices=1)
    t = {k: nc.dram_tensor("in_" + k, v.shape, mybir.dt.from_np(v.dtype), kind="ExternalInput").ap() for k, v in arrays.items()}
    out = nc.dram_tensor("out", (TILES * P, D), F32, kind="ExternalOutput").ap()
    build(nc, t["x"], t["wts"], t["keys"], t["gains"], t["small"], t["sinks"], t["convw"], t["pos"], t["rope0"],
          t["invf"], t["iota"], t["ident"], t["masks"], [t[f"uv{l}"] for l in range(LAYERS)], out)
    got = run_bass_kernel_spmd(nc, [{"in_" + k: v for k, v in arrays.items()}], core_ids=[0]).results[0]["out"]
    return got.reshape(1, TILES * P, D)
```
